# Optimizing a Trainium2 kernel written in Bass

```python
import math
import jax, jax.numpy as jnp
from jax import lax
import numpy as np

D_MODEL = 1024
BATCH = 1
SEQ = 256
DEPTH = 2
DEC_BATCH = 8
DEC_SEQ = 1
PAST_LEN = 2048
PAGE_SIZE = 128

N_EVEN = (DEPTH + 1) // 2
N_ODD = DEPTH // 2
SSD_HEAD_DIM = 64
SSD_HEADS = 16
D_SSD = SSD_HEADS * SSD_HEAD_DIM
SSD_GROUPS = 4
SSD_HEADS_PER_GROUP = SSD_HEADS // SSD_GROUPS
SSD_STATE = 128
SSD_CONV = 4
SSD_CHUNK = 128
SSD_CONV_DIM = D_SSD + 2 * SSD_GROUPS * SSD_STATE
DT_MIN = 0.001
DT_MAX = 0.1
GMLP_CHUNK = 128
GMLP_GROUPS = 8
D_GMLP = D_MODEL
GMLP_GROUP_DIM = D_GMLP // GMLP_GROUPS
IN_DIM = D_SSD + SSD_CONV_DIM + SSD_HEADS + 2 * D_GMLP
MIX_DIM = D_SSD + D_GMLP
D_CONF = D_MODEL
CONF_KERNEL = 31
D_FF = 2816
N_EXPERTS = 8
TOP_K = 2
RMS_EPS = 1e-6
LN_EPS = 1e-5

kernel_name = "hybrid_ssd_gmlp_conformer_moe_step"

def rmsnorm(x, g):
    xf = x.astype(jnp.float32)
    y = xf * lax.rsqrt(jnp.mean(xf * xf, axis=-1, keepdims=True) + RMS_EPS)
    return (y * g.astype(jnp.float32)).astype(x.dtype)

def layernorm(x, g, b):
    xf = x.astype(jnp.float32)
    mu = jnp.mean(xf, axis=-1, keepdims=True)
    var = jnp.mean(jnp.square(xf - mu), axis=-1, keepdims=True)
    y = (xf - mu) * lax.rsqrt(var + LN_EPS) * g.astype(jnp.float32) + b.astype(jnp.float32)
    return y.astype(x.dtype)

def pad_len(a, new_len):
    return jnp.pad(a, [(0, 0), (0, new_len - a.shape[1])] + [(0, 0)] * (a.ndim - 2))

def causal_dwconv(x, buf, w, b):
    xp = jnp.concatenate([buf.astype(x.dtype), x], axis=1)
    y = lax.conv_general_dilated(xp, w[:, None, :].astype(x.dtype), window_strides=(1,), padding='VALID',
                                 dimension_numbers=('NWC', 'WIO', 'NWC'), feature_group_count=x.shape[-1])
    return y + b.astype(x.dtype), xp[:, xp.shape[1] - (w.shape[0] - 1):]

def segsum(a):
    t = a.shape[-1]
    cs = jnp.cumsum(a, axis=-1)
    seg = cs[..., :, None] - cs[..., None, :]
    return jnp.where(jnp.tril(jnp.ones((t, t), dtype=bool)), seg, -jnp.inf)

def ssd_chunked(xdt, a_dt, bm, cm, init_state):
    bsz, L = xdt.shape[:2]
    t = min(L, SSD_CHUNK)
    nc = -(-L // t)
    lp = nc * t
    xc = pad_len(xdt, lp).reshape(bsz, nc, t, SSD_GROUPS, SSD_HEADS_PER_GROUP, SSD_HEAD_DIM)
    ac = pad_len(a_dt, lp).reshape(bsz, nc, t, SSD_GROUPS, SSD_HEADS_PER_GROUP).transpose(0, 3, 4, 1, 2)
    bc = pad_len(bm, lp).reshape(bsz, nc, t, SSD_GROUPS, SSD_STATE)
    cc = pad_len(cm, lp).reshape(bsz, nc, t, SSD_GROUPS, SSD_STATE)
    a_cs = jnp.cumsum(ac, axis=-1)
    decay_in = jnp.exp(segsum(ac))
    cb = jnp.einsum('bclgn,bcsgn->bcgls', cc, bc)
    y_diag = jnp.einsum('bcgls,bgrcls,bcsgrp->bclgrp', cb, decay_in, xc)
    decay_to_end = jnp.exp(a_cs[..., -1:] - a_cs)
    chunk_states = jnp.einsum('bclgn,bgrcl,bclgrp->bcgrpn', bc, decay_to_end, xc)
    chunk_states = jnp.concatenate([init_state[:, None], chunk_states], axis=1)
    a_last = jnp.pad(a_cs[..., -1], [(0, 0), (0, 0), (0, 0), (1, 0)])
    decay_chunk = jnp.exp(segsum(a_last))
    states = jnp.einsum('bgrzc,bcgrpn->bzgrpn', decay_chunk, chunk_states)
    prev_states, final_state = states[:, :-1], states[:, -1]
    y_off = jnp.einsum('bclgn,bcgrpn,bgrcl->bclgrp', cc, prev_states, jnp.exp(a_cs))
    y = (y_diag + y_off).reshape(bsz, lp, SSD_GROUPS, SSD_HEADS_PER_GROUP, SSD_HEAD_DIM)[:, :L]
    return y, final_state

def gated_group_rmsnorm(y, z, g):
    bsz, L, _ = y.shape
    yf = y.astype(jnp.float32) * jax.nn.silu(z.astype(jnp.float32))
    yg = yf.reshape(bsz, L, SSD_GROUPS, D_SSD // SSD_GROUPS)
    yg = yg * lax.rsqrt(jnp.mean(yg * yg, axis=-1, keepdims=True) + RMS_EPS)
    return (yg.reshape(bsz, L, D_SSD) * g.astype(jnp.float32)).astype(z.dtype)

def chunk_gmlp(u, v, ln_g, ln_b, w_s, b_s):
    u = jax.nn.gelu(u)
    v = layernorm(jax.nn.gelu(v), ln_g, ln_b)
    bsz, L, _ = v.shape
    t = min(L, GMLP_CHUNK)
    nc = -(-L // t)
    lp = nc * t
    vp = pad_len(v, lp).reshape(bsz, nc, t, GMLP_GROUPS, GMLP_GROUP_DIM)
    ws = jnp.where(jnp.tril(jnp.ones((t, t), dtype=bool)), w_s[:, :t, :t], 0.0).astype(v.dtype)
    mixed = jnp.einsum('gij,bcjgd->bcigd', ws, vp) + b_s[:, :t].T.astype(v.dtype)[None, None, :, :, None]
    mixed = mixed.reshape(bsz, lp, D_GMLP)[:, :L]
    return u * mixed, v

def swiglu(h, wg, wu, wd):
    return (jax.nn.silu(h @ wg) * (h @ wu)) @ wd

def moe_swiglu(h, router, wg, wu, wd):
    logits = (h @ router).astype(jnp.float32)
    top_v, top_i = lax.top_k(logits, TOP_K)
    gates = jax.nn.softmax(top_v, axis=-1)
    out = jnp.zeros_like(h)
    for e in range(N_EXPERTS):
        gate_e = jnp.sum(jnp.where(top_i == e, gates, 0.0), axis=-1)[..., None].astype(h.dtype)
        out = out + gate_e * swiglu(h, wg[e], wu[e], wd[e])
    return out

def even_mixer(h, ssm_state, conv_buf, p, i):
    bsz, L, _ = h.shape
    f32 = jnp.float32
    proj = h @ p['w_in_even'][i]
    s1 = D_SSD
    s2 = s1 + SSD_CONV_DIM
    s3 = s2 + SSD_HEADS
    s4 = s3 + D_GMLP
    z, xbc, dt_raw, u, v = jnp.split(proj, [s1, s2, s3, s4], axis=-1)
    xbc, new_buf = causal_dwconv(xbc, conv_buf, p['ssd_conv_w'][i], p['ssd_conv_b'][i])
    xbc = jax.nn.silu(xbc)
    xs, bm, cm = jnp.split(xbc, [D_SSD, D_SSD + SSD_GROUPS * SSD_STATE], axis=-1)
    xs = xs.astype(f32).reshape(bsz, L, SSD_GROUPS, SSD_HEADS_PER_GROUP, SSD_HEAD_DIM)
    bm = bm.astype(f32).reshape(bsz, L, SSD_GROUPS, SSD_STATE)
    cm = cm.astype(f32).reshape(bsz, L, SSD_GROUPS, SSD_STATE)
    dt = jax.nn.softplus(dt_raw.astype(f32) + p['ssd_dt_bias'][i].astype(f32))
    dt = dt.reshape(bsz, L, SSD_GROUPS, SSD_HEADS_PER_GROUP)
    a = -jnp.exp(p['ssd_a_log'][i].astype(f32)).reshape(SSD_GROUPS, SSD_HEADS_PER_GROUP)
    init = ssm_state.astype(f32).reshape(bsz, SSD_GROUPS, SSD_HEADS_PER_GROUP, SSD_HEAD_DIM, SSD_STATE)
    y, final = ssd_chunked(xs * dt[..., None], dt * a, bm, cm, init)
    d_skip = p['ssd_d'][i].astype(f32).reshape(SSD_GROUPS, SSD_HEADS_PER_GROUP)[:, :, None]
    y = (y + d_skip * xs).reshape(bsz, L, D_SSD)
    y = gated_group_rmsnorm(y, z, p['ssd_norm'][i])
    g_out, v_rows = chunk_gmlp(u, v, p['gmlp_ln_g'][i], p['gmlp_ln_b'][i], p['gmlp_w_s'][i], p['gmlp_b_s'][i])
    mix = jnp.concatenate([y, g_out], axis=-1) @ p['w_out_even'][i]
    new_state = final.reshape(bsz, SSD_HEADS, SSD_HEAD_DIM, SSD_STATE).astype(ssm_state.dtype)
    return mix, new_state, new_buf.astype(conv_buf.dtype), v_rows

def conformer_conv(h, conv_buf, p, i):
    a = h @ p['conf_w1'][i] + p['conf_b1'][i]
    val, gate = jnp.split(a, 2, axis=-1)
    a = val * jax.nn.sigmoid(gate)
    c, new_buf = causal_dwconv(a, conv_buf, p['conf_dw_w'][i], p['conf_dw_b'][i])
    c = jax.nn.silu(layernorm(c, p['conf_ln_g'][i], p['conf_ln_b'][i]))
    return c @ p['conf_w2'][i] + p['conf_b2'][i], new_buf.astype(conv_buf.dtype)

def trunk(x, ssm_states, ssd_bufs, conf_bufs, p):
    new_ssm, new_ssd_buf, new_conf_buf, v_rows = [], [], [], []
    for layer in range(DEPTH):
        i = layer // 2
        if layer % 2 == 0:
            mix, s, cb, vr = even_mixer(rmsnorm(x, p['norm_mix_even'][i]), ssm_states[i], ssd_bufs[i], p, i)
            new_ssm.append(s)
            new_ssd_buf.append(cb)
            v_rows.append(vr)
            x = x + mix
            x = x + swiglu(rmsnorm(x, p['norm_ffn_even'][i]), p['ffn_w_gate'][i], p['ffn_w_up'][i], p['ffn_w_down'][i])
        else:
            mix, cb = conformer_conv(rmsnorm(x, p['norm_mix_odd'][i]), conf_bufs[i], p, i)
            new_conf_buf.append(cb)
            x = x + mix
            x = x + moe_swiglu(rmsnorm(x, p['norm_ffn_odd'][i]), p['moe_router'][i], p['moe_w_gate'][i],
                               p['moe_w_up'][i], p['moe_w_down'][i])
    y = rmsnorm(x, p['final_norm'])
    return y, jnp.stack(new_ssm), jnp.stack(new_ssd_buf), jnp.stack(new_conf_buf), jnp.stack(v_rows)

def setup_inputs(seed: int = 0) -> dict:
    key = jax.random.key(seed)
    ks = iter(jax.random.split(key, 48))

    def nrm(shape, scale):
        return scale * jax.random.normal(next(ks), shape, jnp.float32)

    def gain(shape):
        return 1.0 + nrm(shape, 0.05)

    dt0 = jnp.exp(jax.random.uniform(next(ks), (N_EVEN, SSD_HEADS), jnp.float32,
                                     minval=math.log(DT_MIN), maxval=math.log(DT_MAX)))
    dt_bias = dt0 + jnp.log(-jnp.expm1(-dt0))
    a_log = jnp.log(jax.random.uniform(next(ks), (N_EVEN, SSD_HEADS), jnp.float32, minval=1.0, maxval=16.0))
    return {
        'x_prompt': nrm((BATCH, SEQ, D_MODEL), 1.0),
        'x_sample': nrm((DEC_BATCH, DEC_SEQ, D_MODEL), 1.0),
        'state_ssm': nrm((N_EVEN, DEC_BATCH, SSD_HEADS, SSD_HEAD_DIM, SSD_STATE), 0.1),
        'state_ssd_conv': nrm((N_EVEN, DEC_BATCH, SSD_CONV - 1, SSD_CONV_DIM), 1.0),
        'state_conf_conv': nrm((N_ODD, DEC_BATCH, CONF_KERNEL - 1, D_CONF), 0.5),
        'norm_mix_even': gain((N_EVEN, D_MODEL)),
        'w_in_even': nrm((N_EVEN, D_MODEL, IN_DIM), D_MODEL ** -0.5),
        'ssd_conv_w': nrm((N_EVEN, SSD_CONV, SSD_CONV_DIM), SSD_CONV ** -0.5),
        'ssd_conv_b': nrm((N_EVEN, SSD_CONV_DIM), 0.02),
        'ssd_dt_bias': dt_bias,
        'ssd_a_log': a_log,
        'ssd_d': gain((N_EVEN, SSD_HEADS)),
        'ssd_norm': gain((N_EVEN, D_SSD)),
        'gmlp_ln_g': gain((N_EVEN, D_GMLP)),
        'gmlp_ln_b': nrm((N_EVEN, D_GMLP), 0.02),
        'gmlp_w_s': nrm((N_EVEN, GMLP_GROUPS, GMLP_CHUNK, GMLP_CHUNK), GMLP_CHUNK ** -0.5),
        'gmlp_b_s': 1.0 + nrm((N_EVEN, GMLP_GROUPS, GMLP_CHUNK), 0.1),
        'w_out_even': nrm((N_EVEN, MIX_DIM, D_MODEL), MIX_DIM ** -0.5),
        'norm_ffn_even': gain((N_EVEN, D_MODEL)),
        'ffn_w_gate': nrm((N_EVEN, D_MODEL, D_FF), D_MODEL ** -0.5),
        'ffn_w_up': nrm((N_EVEN, D_MODEL, D_FF), D_MODEL ** -0.5),
        'ffn_w_down': nrm((N_EVEN, D_FF, D_MODEL), D_FF ** -0.5),
        'norm_mix_odd': gain((N_ODD, D_MODEL)),
        'conf_w1': nrm((N_ODD, D_MODEL, 2 * D_CONF), D_MODEL ** -0.5),
        'conf_b1': nrm((N_ODD, 2 * D_CONF), 0.02),
        'conf_dw_w': nrm((N_ODD, CONF_KERNEL, D_CONF), CONF_KERNEL ** -0.5),
        'conf_dw_b': nrm((N_ODD, D_CONF), 0.02),
        'conf_ln_g': gain((N_ODD, D_CONF)),
        'conf_ln_b': nrm((N_ODD, D_CONF), 0.02),
        'conf_w2': nrm((N_ODD, D_CONF, D_MODEL), D_CONF ** -0.5),
        'conf_b2': nrm((N_ODD, D_MODEL), 0.02),
        'norm_ffn_odd': gain((N_ODD, D_MODEL)),
        'moe_router': nrm((N_ODD, D_MODEL, N_EXPERTS), D_MODEL ** -0.5),
        'moe_w_gate': nrm((N_ODD, N_EXPERTS, D_MODEL, D_FF), D_MODEL ** -0.5),
        'moe_w_up': nrm((N_ODD, N_EXPERTS, D_MODEL, D_FF), D_MODEL ** -0.5),
        'moe_w_down': nrm((N_ODD, N_EXPERTS, D_FF, D_MODEL), D_FF ** -0.5),
        'final_norm': gain((D_MODEL,)),
    }

def reference(x_prompt, x_sample, state_ssm, state_ssd_conv, state_conf_conv,
              norm_mix_even, w_in_even, ssd_conv_w, ssd_conv_b, ssd_dt_bias, ssd_a_log, ssd_d, ssd_norm,
              gmlp_ln_g, gmlp_ln_b, gmlp_w_s, gmlp_b_s, w_out_even,
              norm_ffn_even, ffn_w_gate, ffn_w_up, ffn_w_down,
              norm_mix_odd, conf_w1, conf_b1, conf_dw_w, conf_dw_b, conf_ln_g, conf_ln_b, conf_w2, conf_b2,
              norm_ffn_odd, moe_router, moe_w_gate, moe_w_up, moe_w_down, final_norm):
    p = dict(norm_mix_even=norm_mix_even, w_in_even=w_in_even, ssd_conv_w=ssd_conv_w, ssd_conv_b=ssd_conv_b,
             ssd_dt_bias=ssd_dt_bias, ssd_a_log=ssd_a_log, ssd_d=ssd_d, ssd_norm=ssd_norm,
             gmlp_ln_g=gmlp_ln_g, gmlp_ln_b=gmlp_ln_b, gmlp_w_s=gmlp_w_s, gmlp_b_s=gmlp_b_s,
             w_out_even=w_out_even, norm_ffn_even=norm_ffn_even, ffn_w_gate=ffn_w_gate, ffn_w_up=ffn_w_up,
             ffn_w_down=ffn_w_down, norm_mix_odd=norm_mix_odd, conf_w1=conf_w1, conf_b1=conf_b1,
             conf_dw_w=conf_dw_w, conf_dw_b=conf_dw_b, conf_ln_g=conf_ln_g, conf_ln_b=conf_ln_b,
             conf_w2=conf_w2, conf_b2=conf_b2, norm_ffn_odd=norm_ffn_odd, moe_router=moe_router,
             moe_w_gate=moe_w_gate, moe_w_up=moe_w_up, moe_w_down=moe_w_down, final_norm=final_norm)
    bp = x_prompt.shape[0]
    ssm0 = jnp.zeros((N_EVEN, bp) + state_ssm.shape[2:], state_ssm.dtype)
    ssd_buf0 = jnp.zeros((N_EVEN, bp) + state_ssd_conv.shape[2:], state_ssd_conv.dtype)
    conf_buf0 = jnp.zeros((N_ODD, bp) + state_conf_conv.shape[2:], state_conf_conv.dtype)
    y_prompt, ssm_p, ssd_conv_p, conf_conv_p, _v_prompt = trunk(x_prompt, ssm0, ssd_buf0, conf_buf0, p)
    y_sample, ssm_s, ssd_conv_s, conf_conv_s, gmlp_v_s = trunk(x_sample, state_ssm, state_ssd_conv,
                                                               state_conf_conv, p)
    return (y_prompt, y_sample, ssm_p, ssd_conv_p, conf_conv_p, ssm_s, ssd_conv_s, conf_conv_s, gmlp_v_s)


_drawn_inputs = setup_inputs


def setup_inputs(seed=0):
    import zlib

    import numpy as np

    out = dict(_drawn_inputs(seed))
    spreads = {}
    factors = {'gmlp_ln_b': 2.799, 'conf_ln_b': 3.323}
    for name, (base, spread) in spreads.items():
        noise = np.random.default_rng([zlib.crc32(name.encode()), seed]).standard_normal(out[name].shape)
        drawn = base * np.exp(spread * noise) if base else spread * noise
        out[name] = __import__('jax').numpy.asarray(drawn.astype(out[name].dtype))
    for name, factor in factors.items():
        out[name] = (out[name] * factor).astype(out[name].dtype)
    return out
```

```python
from contextlib import ExitStack

import concourse.bass as bass
from concourse import mybir

F32 = mybir.dt.float32
I32 = mybir.dt.int32
ALU = mybir.AluOpType
ACT = mybir.ActivationFunctionType
AX = mybir.AxisListType

P = 128
D = 1024
DC = D // P
TP = 256
TS = 8
T = TP + TS
BLK = 3
ROWS = (P, P, TS)
XBC = 16
HEADS = 16
HD = 64
GR = 4
NST = 128
FF = 2816
FC = FF // P
EXP = 8
CAP = 112
ROUNDS = 3
KC = 31
POOL_CHUNKS = (0,)
PE_CHUNKS = (3, 6)
DVE_CHUNKS = (1, 2, 4, 5, 7)
DIAGS = 40
ITEMS = EXP * ROUNDS
LOADS = FF // 256
RMS_EPS = 1e-6
LN_EPS = 1e-5
NEG_BIG = -1e30

PARAMS = (("norm_mix_even", 8), ("ssd_conv_b", 16), ("ssd_norm", 8), ("gmlp_ln_g", 8), ("gmlp_ln_b", 8),
          ("norm_ffn_even", 8), ("norm_mix_odd", 8), ("conf_b1", 16), ("conf_dw_b", 8), ("conf_ln_g", 8),
          ("conf_ln_b", 8), ("conf_b2", 8), ("norm_ffn_odd", 8))
COL = {}
for _name, _n in PARAMS:
    COL[_name] = sum(n for _, n in PARAMS[:len(COL)])
PROWS = sum(n for _, n in PARAMS)
COL["ssd_conv_w"] = 128
COL["conf_dw_w"] = 256


def psum_tiles():
    out = []

    def add(name, *drained):
        out.append((name, drained))

    for i in range(6):
        add(("xT", i), ("xT_ready", i + 1))
    add("par", ("par_ready", 2))
    add("cols", ("cols_ready", 1))
    for i in range(2):
        add(("wsT", i), ("wsT_ready", i + 1))
    add("cbufT", ("cbuf_ready", 1))
    for c in range(XBC):
        add(("xbc", c), ("raw_ready", c + 1))
    add("dt", ("dt_raw", 2))
    for i in range(4):
        add(("crow", i), ("crow_ready", i + 1))
    for c in range(DC):
        add(("v", c), ("gv_ready", c + 1))
        if c == 3:
            for i in range(2):
                add(("sBC", i), ("sbc_ready", i + 1))
            add("dtT", ("dtT_ready", 1))
            add("dtrep", ("dtrep_ready", 1))
        if c >= 4:
            for j in range(2):
                add(("BC", 2 * c - 8 + j), ("bc_ready", 2 * c - 8 + j + 1))
    for c in range(DC):
        add(("u", c), ("u_ready", c + 1))
        if c < 4:
            for j in range(2):
                add(("BC", 2 * c + 8 + j), ("bc_ready", 2 * c + 8 + j + 1))
    add("cs", ("cs_ready", 1))
    for i in range(4):
        add(("xtok", i), ("xdt_ready", i + 1))
    for q in range(2):
        add(("Btok", q), ("btok_ready", q + 1))
    for i in range(2):
        add(("vrow", i), ("vrow_ready", i + 1))
    for i in range(4):
        add(("vtok", i), ("vtok_ready", i + 1))
    for g in range(DC):
        add(("mx", g), ("gout_ready", 2 * g + 2))
    for i in range(2):
        add(("prevT", i), ("prevT_ready", i + 1))
    for i in range(9):
        if i < 8:
            add(("z", i), ("z_raw", i + 1))
            add(("cb", i), ("m_ready", i + 1))
            add(("cr", i), *((("seg_ready", 4 * i + 4),) + ((("ecs_ready", i - 3),) if i >= 4 else ())))
        if i >= 1:
            add(("y", i - 1), ("y_ready", 2 * i))
    for i in range(2):
        add(("fst", i), ("fst_ready", i + 1))
    for g in range(GR):
        add(("gn", g), ("gn_read", g + 1))
    for c in range(DC):
        add(("wo", c), ("res_ready", c + 1))
    for f in range(FC):
        add(("fg", f), ("fg_ready", f + 1))
        add(("fu", f), ("fh_ready", f + 1))
    for c in range(DC):
        add(("fd", c), ("res_ready", 8 + c + 1))
    for i in range(4):
        add(("cbT", i), ("ccb_ready", i + 1))
    for c in range(DC):
        add(("cv", c), ("ca_ready", c + 1))
        add(("cg", c), ("sg_ready", c + 1))
    for i in range(2):
        add(("crw", i), ("crw_ready", i + 1))
    for n, c in enumerate(PE_CHUNKS):
        add(("taps", c), ("cc_taps", n + 1))
    for c in range(DC):
        add(("w2", c), ("res_ready", 16 + c + 1))
    for i in range(6):
        add(("xt2", i), ("acc_ready", i + 1))
    add("lg", ("lg_ready", 2))
    for i in range(6):
        add(("ht", i), ("htok_ready", i + 1))
    add("pos", ("pos_ready", 1))
    return out


def build(nc, i, o):
    TILES = psum_tiles()
    NUM = {name: n for n, (name, _) in enumerate(TILES)}
    RING = 7
    ctx = ExitStack()
    with ctx:
        def sb(name, cols, dt=F32, parts=P):
            return ctx.enter_context(nc.sbuf_tensor(name, [parts, cols], dt))

        sems = {}

        def sem(name):
            if name not in sems:
                sems[name] = ctx.enter_context(nc.semaphore(name))
            return sems[name]

        for _, drained in TILES:
            for s, _ in drained:
                sem(s)

        ring = sb("ring", 4 * 6144)
        XTt = sb("XTt", DC * T)
        Ht = sb("Ht", DC * T)
        XT = XTt[:, :].rearrange("p (c t) -> p c t", c=DC)
        H = Ht[:, :].rearrange("p (c t) -> p c t", c=DC)
        ident = sb("ident", P)
        ones = sb("ones", P)
        upper = sb("upper", P)
        supper = sb("supper", P)
        negm = sb("negm", P)
        bselt = sb("bselt", TS * P, parts=TS)
        bsel = bselt[0:TS, :].rearrange("k (b m) -> k b m", b=TS)
        par = sb("par", 512)
        iota = sb("iota", CAP)
        rstd = sb("rstd", T)
        muS = sb("muS", T)
        eps = sb("eps", 2)
        bsrow = sb("bsrow", DC * P, parts=1)
        row16 = sb("row16", 16, parts=1)
        region = sb("region", 20800)

        def reg(at, n):
            return region[:, at:at + n]

        rawt = reg(0, XBC * (T + 3))
        raw = rawt.rearrange("p (c t) -> p c t", c=XBC)
        BCr = reg(0, 2048).rearrange("p (s n) -> p s n", s=2)
        t2 = reg(2048, 1024)
        t3 = reg(3072, 1024)
        xct = reg(4272, XBC * T)
        xc = xct.rearrange("p (c t) -> p c t", c=XBC)
        GV = reg(8496, DC * T).rearrange("p (c t) -> p c t", c=DC)
        SQ0 = GV
        st = reg(10608, 4096).rearrange("p (b c n) -> p b c n", b=4, c=DC)
        xtk = reg(10608, 3072).rearrange("p (k d) -> p k d", k=BLK)
        wsT = reg(14704, 1024)
        cbuf = reg(15728, 384).rearrange("p (c k) -> p c k", c=XBC)
        small = reg(16112, 464)
        dtx, dtm, dta, adt = (small[:, 48 * k:48 * k + 48] for k in range(4))
        ncs = small[:, 192:224]
        tot = small[:, 224:256]
        wend = small[:, 256:288]
        wfin = small[:, 288:304]
        dbias = small[:, 304:320]
        arep = small[:, 320:336]
        dfe = small[:, 336:360]
        dts = small[:, 360:376]
        mixt = reg(16576, XBC * T)
        mix = mixt.rearrange("p (c t) -> p c t", c=XBC)
        Z = mix[:, 0:DC, :]
        U = mix[:, DC:XBC, :]
        vtok = mixt[:, 0:2048].rearrange("p (q d) -> p q d", q=2)
        cbrows = mixt[0:24, 0:2048]
        wsn = mixt[:, 2048:3072].rearrange("p (g j) -> p g j", g=DC)
        prow = mixt[:, 3072:3584].rearrange("p (k r) -> p k r", k=4)
        sdt = sb("sdt", 320)
        dtrep = sdt[:, 0:128]

        def scr(at, n):
            return ring[:, 12288 + at:12288 + at + n]

        xdt = scr(0, 2048).rearrange("p (q d) -> p q d", q=2)
        xw0 = scr(2048, 1024)
        fsto = scr(2048, 1024)
        xf = scr(3072, 2048).rearrange("p (q d) -> p q d", q=2)
        crows = scr(3072, 2048)[0:11, :]
        Btok = scr(5120, 1024).rearrange("p (q d) -> p q d", q=2)
        prevT = scr(6144, 1024)
        dec = scr(7168, 1024).rearrange("p (s r l) -> p s r l", s=2, r=4)
        Mt = scr(8192, 1024).rearrange("p (s r l) -> p s r l", s=2, r=4)
        ecs = scr(9216, 1024).rearrange("p (s r l) -> p s r l", s=2, r=4)
        Cs = scr(10240, 1024).rearrange("p (s r l) -> p s r l", s=2, r=4)
        SQ1 = scr(7168, DC * T).rearrange("p (c t) -> p c t", c=DC)
        esel = scr(11264, 1024)[0:HEADS, :].rearrange("h (c m) -> h c m", c=DC)
        vrows = scr(11264, 1024)[0:TS, :]
        sBC = sb("sBC", 1024, parts=TS)

        HT = reg(0, FC * T).rearrange("p (f t) -> p f t", f=FC)
        diag = reg(0, DIAGS * P).rearrange("p (s m) -> p s m", s=DIAGS)
        SQ2 = reg(5808, DC * T).rearrange("p (c t) -> p c t", c=DC)
        CA0 = 7920
        ca = reg(CA0, DC * (T + 30)).rearrange("p (c t) -> p c t", c=DC)
        ccb = reg(CA0 + 2352, 1920)
        ccbv = ccb.rearrange("p (c b k) -> p c b k", c=DC, b=TS)
        ccr = reg(CA0 + 4272, 2048).rearrange("p (s d) -> p s d", s=2)
        ctmp = reg(CA0 + 6320, 1920)
        CC = reg(CA0 + 8240, DC * T).rearrange("p (c t) -> p c t", c=DC)
        crw = reg(CA0 + 10352, 1024)
        sgb = reg(CA0 + 11376, 2 * T).rearrange("p (s t) -> p s t", s=2)
        siluG = reg(CA0 + 11904, 2 * T).rearrange("p (s t) -> p s t", s=2)
        ctail = reg(CA0 + 12432, 64)
        ptmp = siluG.rearrange("p s t -> p (s t)")[:, 0:2 * TP].rearrange("p (s t) -> p s t", s=2)

        htok = reg(0, 3072).rearrange("p (k d) -> p k d", k=BLK)
        acc = reg(CA0, 3072).rearrange("p (k d) -> p k d", k=BLK)
        ysb = reg(CA0 + 3072, 1024)
        xg = reg(CA0 + 4096, DC * CAP).rearrange("p (c j) -> p c j", c=DC)
        Sel = reg(CA0 + 4992, BLK * CAP).rearrange("p (k j) -> p k j", k=BLK)
        SelG = reg(CA0 + 5328, BLK * CAP).rearrange("p (k j) -> p k j", k=BLK)
        SelGT = reg(CA0 + 5664, BLK * P)
        hact = reg(CA0 + 6048, 4 * CAP).rearrange("p (s f j) -> p s f j", s=2, f=2)
        sgm = reg(CA0 + 6496, 4 * CAP).rearrange("p (s f j) -> p s f j", s=2, f=2)
        rt = reg(CA0 + 6944, 1152)
        L = rt[:, 0:24]
        rank = rt[:, 24:48]
        m1 = rt[:, 48:72]
        m2 = rt[:, 72:96]
        mask = rt[:, 96:120]
        tmp24 = rt[:, 120:144]
        v12 = rt[:, 144:150]
        gt12 = rt[:, 150:162]
        valid = rt[:, 162:165]
        cnt = rt[:, 165:173]
        nrf = rt[:, 173:176]
        cmp1 = rt[:, 192:384]
        cmp2 = rt[:, 384:576]
        ltm = rt[:, 576:640]
        posm = rt[:, 640:664]
        gate = rt[:, 664:688]
        NT = ITEMS + 2
        ptab = rt[:, 700:700 + 3 * NT].rearrange("p (k n) -> p k n", k=BLK)
        gtab = rt[:, 800:800 + 3 * NT].rearrange("p (k n) -> p k n", k=BLK)
        ssum = rt[:, 900:903]
        fgain = reg(CA0 + 8096, 1024)
        fsq = reg(3072, 1024)
        tint = sb("tint", 2, I32, parts=1)

        psum = [ctx.enter_context(nc.psum_tensor(f"ps{b}", [P, 512], F32)) for b in range(8)]
        STAT = psum[7]

        def tile(name):
            return psum[NUM[name] % RING]

        def filled(eng, name):
            eng.wait_ge(sem("psum_full"), NUM[name] + 1)

        small_steps = [("in", 1024 + 512 * k) for k in range(4)] + [("in", 4112), ("in", 4624), ("in", 3088),
                                                                   ("in", 3600), ("in", 0), ("in", 512)]
        small_steps += [("out", 256 * k) for k in range(4)]
        big_steps = [("ffn", k) for k in range(LOADS)] + [("down", k) for k in range(4)]
        big_steps += [("conf1", k) for k in range(4)] + [("conf2", k) for k in range(2)]
        NSM = len(small_steps)
        NBIG = len(big_steps)
        LAST_TILE = [("xbc", 4 * k + 3) for k in range(4)] + [(x, 4 * k + 3) for x in "vuz" for k in range(2)]
        LAST_TILE += [("wo", 2 * k + 1) for k in range(4)] + [("fu", 2 * k + 1) for k in range(LOADS)]
        LAST_TILE += [("fd", 2 * k + 1) for k in range(4)] + [("cg", 2 * k + 1) for k in range(4)]
        LAST_TILE += [("w2", 4 * k + 3) for k in range(2)]
        assert len(LAST_TILE) == NSM + NBIG
        DMAS = {"in": 1, "out": 1, "ffn": 2, "down": 1, "conf1": 2, "conf2": 1}
        STEP = {}
        arrived = {}
        for n, s in enumerate(small_steps + big_steps):
            slot = n % 3 if n < NSM else (n - NSM + 2) % 4
            name = f"w_small{slot}" if n < NSM else f"w_slot{slot}"
            arrived[name] = arrived.get(name, 0) + 16 * DMAS[s[0]]
            STEP[s] = (n, slot, name, arrived[name])
        SLOT_BASE = [arrived[f"w_slot{s}"] for s in range(4)]
        SLOT_USES = [len(range(s, LOADS, 4)) for s in range(4)]
        for s in range(4):
            sem(f"w_slot{s}")
        for s in range(3):
            sem(f"w_small{s}")

        def wview(step):
            n, slot, _, _ = STEP[step]
            return ring[:, 4096 * slot:4096 * (slot + 1)] if n < NSM else ring[:, 6144 * slot:6144 * (slot + 1)]

        wdt = sb("wdt", DC * 16)
        wrt = sb("wrt", DC * EXP)
        bc = lambda ap, axis, shape: ap.unsqueeze(axis).broadcast_to(shape)

        block = ctx.enter_context(nc.Block())

        @block.sync
        def _(sp):
            w_in = i["w_in_even"][0].rearrange("(c p) n -> p c n", p=P)
            w_out = i["w_out_even"][0].rearrange("(c p) n -> p c n", p=P)
            w_g = i["ffn_w_gate"][0].rearrange("(c p) n -> p c n", p=P)
            w_u = i["ffn_w_up"][0].rearrange("(c p) n -> p c n", p=P)
            w_d = i["ffn_w_down"][0].rearrange("(c p) n -> p c n", p=P)
            c_1 = i["conf_w1"][0].rearrange("(c p) n -> p c n", p=P)
            c_2 = i["conf_w2"][0].rearrange("(c p) n -> p c n", p=P)
            sp.wait_ge(sem("prow_zero"), 1)
            for name, n in PARAMS:
                sp.dma_start(prow[COL[name]:COL[name] + n, 0, :],
                              i[name][0].rearrange("(c p) -> c p", p=P)).then_inc(sem("par_loaded"), 16)
            sp.dma_start(prow[0:64, 1, :], i["ssd_conv_w"][0].rearrange("k (c p) -> (k c) p", p=P)).then_inc(
                sem("par_loaded"), 16)
            dw = i["conf_dw_w"][0].rearrange("k (c p) -> (k c) p", p=P)
            sp.dma_start(prow[:, 2, :], dw[0:128]).then_inc(sem("par_loaded"), 16)
            sp.dma_start(prow[0:120, 3, :], dw[128:248]).then_inc(sem("par_loaded"), 16)
            sp.dma_start(wsn, i["gmlp_w_s"][0].rearrange("g i j -> i g j")).then_inc(sem("ws_loaded"), 16)
            sp.dma_start(cbrows, i["state_ssd_conv"][0].rearrange("b k n -> (b k) n")).then_inc(sem("cb_loaded"), 16)
            sp.dma_start(row16[0:1, 0:8], i["gmlp_w_s"][0, :, 0, 0:1].rearrange("g a -> a g"),
                          allow_slow_non_contiguous=True).then_inc(sem("row_loaded"), 16)
            sp.dma_start(row16[0:1, 8:16], i["gmlp_b_s"][0, :, 0:1].rearrange("g a -> a g"),
                          allow_slow_non_contiguous=True).then_inc(sem("row_loaded"), 16)
            sp.dma_start(dts[0:HEADS, 0:1], i["ssd_d"].rearrange("a h -> h a"),
                          allow_slow_non_contiguous=True).then_inc(sem("row_loaded"), 16)
            sp.dma_start(dbias, i["ssd_dt_bias"].broadcast_to([P, HEADS])).then_inc(sem("dtp_loaded"), 16)
            sp.dma_start(arep, i["ssd_a_log"].broadcast_to([P, HEADS])).then_inc(sem("dtp_loaded"), 16)
            for s in small_steps + big_steps:
                n, slot, name, _ = STEP[s]
                dst = wview(s)
                if n == 0:
                    sp.wait_ge(sem("x_loaded"), 48)
                if n < NSM:
                    if n >= 3:
                        filled(sp, LAST_TILE[n - 3])
                elif n < NSM + 2:
                    sp.wait_ge(sem("fst_stored"), 16)
                    sp.wait_ge(sem("vrow_stored"), 16)
                    sp.wait_ge(sem("crow_stored"), 32)
                    filled(sp, ("gn", GR - 1))
                elif n < NSM + 4:
                    filled(sp, LAST_TILE[NSM - 1])
                else:
                    filled(sp, LAST_TILE[n - 4])
                if s[0] == "in":
                    pieces = [(dst.rearrange("p (c n) -> p c n", c=DC), w_in[:, :, s[1]:s[1] + 512])]
                elif s[0] == "out":
                    pieces = [(dst.rearrange("p (c n) -> p c n", c=XBC), w_out[:, :, s[1]:s[1] + 256])]
                elif s[0] == "ffn":
                    pieces = [(dst[:, 2048 * k:2048 * (k + 1)].rearrange("p (c n) -> p c n", c=DC),
                               w[:, :, 256 * s[1]:256 * (s[1] + 1)]) for k, w in enumerate((w_g, w_u))]
                elif s[0] == "down":
                    pieces = [(dst[:, 0:FC * 256].rearrange("p (c n) -> p c n", c=FC),
                               w_d[:, :, 256 * s[1]:256 * (s[1] + 1)])]
                elif s[0] == "conf1":
                    pieces = [(dst[:, 2048 * k:2048 * (k + 1)].rearrange("p (c n) -> p c n", c=DC),
                               c_1[:, :, D * k + 256 * s[1]:D * k + 256 * (s[1] + 1)]) for k in range(2)]
                else:
                    pieces = [(dst[:, 0:4096].rearrange("p (c n) -> p c n", c=DC),
                               c_2[:, :, 512 * s[1]:512 * (s[1] + 1)])]
                for to, of in pieces:
                    sp.dma_start(to, of).then_inc(sem(name), 16)
                if n == 0:
                    sp.dma_start(wdt[:, :].rearrange("p (c n) -> p c n", c=DC),
                                 w_in[:, :, 3072:3088]).then_inc(sem("wdt_loaded"), 16)
                if n == 2:
                    sp.dma_start(wrt[:, :].rearrange("p (c e) -> p c e", c=DC),
                                  i["moe_router"][0].rearrange("(c p) e -> p c e", p=P)).then_inc(sem("router_loaded"), 16)
                    sp.dma_start(bsrow[0:1, :], i["gmlp_b_s"].rearrange("a g t -> a (g t)")).then_inc(sem("bs_loaded"), 16)
                    sp.dma_start(o["ssd_conv_sample"][0, :, 0:2, :], i["state_ssd_conv"][0, :, 1:3, :]).then_inc(
                        sem("moved"), 16)
                    sp.dma_start(o["conf_conv_sample"][0, :, 0:29, :], i["state_conf_conv"][0, :, 1:30, :]).then_inc(
                        sem("moved"), 16)

            def expert(e, t, first=False):
                g = i["moe_w_gate"][0, bass.ds(e, 1)].rearrange("a (c p) n -> p (a c) n", p=P)
                u = i["moe_w_up"][0, bass.ds(e, 1)].rearrange("a (c p) n -> p (a c) n", p=P)
                d = i["moe_w_down"][0, bass.ds(e, 1)].rearrange("a (f p) n -> p (a f) n", p=P)
                for k in range(LOADS):
                    slot = k % 4
                    last = k - 4 if k >= 4 else ((LOADS - 1 - k) // 4 * 4 + k) - LOADS
                    if first and last < 0:
                        filled(sp, LAST_TILE[last])
                    else:
                        sp.wait_ge(sem("w_used"), t * LOADS + (last + 1))
                    dst = ring[:, 6144 * slot:6144 * (slot + 1)]
                    for j, (to, of) in enumerate((
                            (dst[:, 0:2048].rearrange("p (c n) -> p c n", c=DC), g[:, :, 256 * k:256 * (k + 1)]),
                            (dst[:, 2048:4096].rearrange("p (c n) -> p c n", c=DC), u[:, :, 256 * k:256 * (k + 1)]),
                            (dst[:, 4096:6144].rearrange("p (f n) -> p f n", f=2), d[:, 2 * k:2 * k + 2, :]))):
                        sp.dma_start(to, of).then_inc(sem(f"w_slot{slot}"), 16)

            expert(0, 0, first=True)
            with sp.Fori(1, EXP) as e:
                expert(e, e)
            sp.wait_ge(sem("rounds_ready"), 1)
            rounds = sp.value_load(tint[0:1, 1:2], min_val=1, max_val=ROUNDS)
            with sp.If(rounds > 1):
                with sp.Fori(1, rounds) as r:
                    with sp.Fori(0, EXP) as e:
                        expert(e, r * EXP + e)

        @block.gpsimd
        def _(pool):
            g = nc.gpsimd
            order = [0]

            def then(ins):
                order[0] += 1
                ins.then_inc(sem("pool_step"), 1)
                pool.wait_ge(sem("pool_step"), order[0])

            then(g.memset(ident[:, :], 0.0))
            g.affine_select(out=ident[:, :], in_=ident[:, :], compare_op=ALU.not_equal, fill=1.0, base=0,
                            pattern=[[-1, P]], channel_multiplier=1).then_inc(sem("ident_ready"), 1)
            g.memset(ones[:, :], 1.0).then_inc(sem("ones_ready"), 1)
            then(g.memset(esel, 0.0))
            g.affine_select(out=esel.rearrange("h c (s m) -> h c s m", s=2),
                            in_=esel.rearrange("h c (s m) -> h c s m", s=2), compare_op=ALU.not_equal, fill=1.0,
                            base=0, pattern=[[-2, DC], [-1, 2], [0, HD]],
                            channel_multiplier=1).then_inc(sem("esel_ready"), 1)
            then(g.memset(bsel, 0.0))
            g.affine_select(out=bsel, in_=bsel, compare_op=ALU.not_equal, fill=1.0, base=0,
                            pattern=[[-1, TS], [0, P]], channel_multiplier=1).then_inc(sem("const_ready"), 1)
            then(g.memset(upper[:, :], 1.0))
            g.affine_select(out=upper[:, :], in_=upper[:, :], compare_op=ALU.is_ge, fill=0.0, base=0,
                            pattern=[[1, P]], channel_multiplier=-1).then_inc(sem("const_ready"), 1)
            then(g.memset(supper[:, :], 1.0))
            g.affine_select(out=supper[:, :], in_=supper[:, :], compare_op=ALU.is_gt, fill=0.0, base=0,
                            pattern=[[1, P]], channel_multiplier=-1).then_inc(sem("const_ready"), 1)
            then(g.memset(negm[:, :], 0.0))
            g.affine_select(out=negm[:, :], in_=negm[:, :], compare_op=ALU.is_ge, fill=NEG_BIG, base=0,
                            pattern=[[1, P]], channel_multiplier=-1).then_inc(sem("const_ready"), 1)
            g.iota(iota[:, :], pattern=[[1, CAP]], base=0, channel_multiplier=0,
                   allow_small_or_imprecise_dtypes=True).then_inc(sem("const_ready"), 1)

            pool.wait_ge(sem("ws_loaded"), 16)
            g.affine_select(out=wsn, in_=wsn, compare_op=ALU.is_ge, fill=0.0, base=0,
                            pattern=[[0, DC], [-1, P]], channel_multiplier=1).then_inc(sem("wsn_ready"), 1)

            sdram = i["state_ssm"][0].rearrange("b (c r) p n -> (r p) b c n", r=2)
            odram = o["ssm_sample"][0].rearrange("b (c r) p n -> (r p) b c n", r=2)

            def load_state(b):
                pool.dma_start(st[:, b % 4], sdram[:, b]).then_inc(sem(f"st_loaded{b % 4}"), 16)

            pool.wait_ge(sem("xT_ready"), 6)
            for b in range(4):
                load_state(b)
            pool.wait_ge(sem("dtrep_ready"), 1)
            drv = dtrep.rearrange("p (c k) -> p c k", c=DC)

            def decay(b):
                pool.wait_ge(sem(f"st_loaded{b % 4}"), 16 * (b // 4 + 1))
                s = st[:, b % 4]
                g.tensor_tensor(s, s, bc(drv[:, :, 8 + b], 2, [P, DC, NST]), ALU.mult).then_inc(sem("st_decayed"), 1)

            decay(0)
            decay(1)
            for b in range(TS):
                pool.wait_ge(sem("st_new"), b + 1)
                pool.dma_start(odram[:, b], st[:, b % 4]).then_inc(sem(f"st_stored{b % 4}"), 16)
                if 1 <= b <= 4:
                    pool.wait_ge(sem(f"st_stored{b - 1}"), 16)
                    pool.wait_ge(sem("sy_mul"), b)
                    load_state(b + 3)
                if b + 2 < TS:
                    decay(b + 2)

            pool.wait_ge(sem("ccb_ready"), 4)
            pool.wait_ge(sem("par_ready"), 2)
            wt = par[:, 256:256 + 240].rearrange("p (k c) -> p c k", c=DC)
            for c in range(DC):
                last = g.tensor_tensor(ctmp[:, 240 * c:240 * (c + 1)].rearrange("p (b k) -> p b k", b=TS), ccbv[:, c],
                                       bc(wt[:, c, :], 1, [P, TS, 30]), ALU.mult)
            last.then_inc(sem("ctmp_ready"), 1)
            for n, c in enumerate(POOL_CHUNKS):
                pool.wait_ge(sem("ca_ready"), c + 1)
                dst = CC[:, c, 0:TP]
                w = [par[:, COL["conf_dw_w"] + 8 * k + c:COL["conf_dw_w"] + 8 * k + c + 1] for k in range(KC)]
                b = COL["conf_dw_b"] + c
                then(g.tensor_scalar(dst, ca[:, c, 0:TP], w[0], par[:, b:b + 1], ALU.mult, ALU.add))
                for k in range(1, KC):
                    then(g.tensor_scalar(ptmp[:, k % 2], ca[:, c, k:k + TP], w[k], 1.0, ALU.mult, ALU.mult))
                    ins = g.tensor_tensor(dst, dst, ptmp[:, k % 2], ALU.add)
                    if k < KC - 1:
                        then(ins)
                ins.then_inc(sem("cc_pool"), 1)

            pool.wait_ge(sem("res_ready"), 24)
            then(g.memset(ltm, 1.0))
            g.affine_select(out=ltm.rearrange("p (e j) -> p e j", e=EXP), in_=ltm.rearrange("p (e j) -> p e j", e=EXP),
                            compare_op=ALU.is_gt, fill=0.0, base=0, pattern=[[1, EXP], [-1, EXP]],
                            channel_multiplier=0).then_inc(sem("route_const"), 1)
            then(g.memset(valid, 1.0))
            g.affine_select(out=valid[:, 2:3], in_=valid[:, 2:3], compare_op=ALU.is_gt, fill=0.0, base=TS,
                            pattern=[[0, 1]], channel_multiplier=-1).then_inc(sem("route_const"), 1)
            pool.dma_start(fgain[:, :], i["final_norm"].rearrange("(a n) -> a n", a=1).broadcast_to([P, D])).then_inc(
                sem("fgain_loaded"), 16)

            for b in range(4):
                pool.wait_ge(sem(f"st_stored{b}"), 32)
            pool.wait_ge(sem("crow_stored"), 32)
            pool.wait_ge(sem("moved"), 32)
            pool.wait_ge(sem("vrow_stored"), 16)
            pool.wait_ge(sem("fst_stored"), 16)
            pool.wait_ge(sem("crw_stored"), 32)
            pool.wait_ge(sem("y_stored"), 48)

        @block.scalar
        def _(act):
            a = nc.scalar
            xp = i["x_prompt"][0].rearrange("(k p) d -> p k d", p=P)
            act.dma_start(xtk[:, 0, :], xp[:, 0]).then_inc(sem("x_loaded"), 16)
            act.dma_start(xtk[:, 1, :], xp[:, 1]).then_inc(sem("x_loaded"), 16)
            act.dma_start(xtk[0:TS, 2, :], i["x_sample"].rearrange("b s d -> (b s) d")).then_inc(sem("x_loaded"), 16)
            def square(k, c, SQ):
                if k == 0:
                    act.wait_ge(sem("xT_ready"), 6)
                else:
                    act.wait_ge(sem("res_ready"), 8 * (k - 1) + c + 1)
                a.activation(SQ[:, c, :], XT[:, c, :], ACT.Square).then_inc(sem("sq_ready"), 1)

            def root(name, e):
                act.wait_ge(sem("stat_full"), STATS.index(name) + 1)
                a.activation(rstd[:, :], STAT[:, 0:T], ACT.Sqrt, scale=1.0 / D, bias=eps[:, e:e + 1]).then_inc(
                    sem("stat_read"), 1)

            for c in range(DC):
                square(0, c, SQ0)
            act.wait_ge(sem("eps_ready"), 2)
            root("norm0", 0)
            act.wait_ge(sem("wsn_ready"), 1)
            for k in range(2):
                filled(act, ("wsT", k))
                a.activation(wsT[:, 512 * k:512 * (k + 1)], tile(("wsT", k))[:, :], ACT.Copy).then_inc(
                    sem("wsT_ready"), 1)
            filled(act, "cbufT")
            a.activation(cbuf, tile("cbufT")[:, 0:384].rearrange("p (c k) -> p c k", c=XBC), ACT.Copy).then_inc(
                sem("cbuf_ready"), 1)

            for c in range(XBC + 2):
                if c < XBC:
                    filled(act, ("xbc", c))
                    a.activation(raw[:, c, 3:3 + T], tile(("xbc", c))[:, 0:T], ACT.Copy).then_inc(sem("raw_ready"), 1)
                if c >= 2:
                    act.wait_ge(sem("conv_ready"), c - 1)
                    a.activation(xc[:, c - 2, 0:TP], xc[:, c - 2, 0:TP], ACT.Silu).then_inc(sem("xc_ready"), 1)
            act.wait_ge(sem("convs_ready"), 1)
            a.activation(xc[:, :, TP:T], xc[:, :, TP:T], ACT.Silu).then_inc(sem("xc_ready"), 1)
            act.wait_ge(sem("dt_raw"), 2)
            a.activation(dtm, dtx, ACT.Abs).then_inc(sem("dt_act"), 1)
            act.wait_ge(sem("dt_act"), 1)
            a.activation(dtm, dtm, ACT.Exp, scale=-1.0).then_inc(sem("dt_act"), 1)
            act.wait_ge(sem("dt_act"), 2)
            a.activation(dtm, dtm, ACT.Ln, bias=ones[:, 0:1]).then_inc(sem("dt_act"), 1)
            act.wait_ge(sem("dtp_loaded"), 32)
            a.activation(arep, arep, ACT.Exp).then_inc(sem("arep_exp"), 1)
            for k in range(4):
                filled(act, ("crow", k))
                a.activation(crows[:, 512 * k:512 * (k + 1)], tile(("crow", k))[0:11, :], ACT.Copy).then_inc(
                    sem("crow_ready"), 1)
            act.wait_ge(sem("crow_ready"), 4)
            act.dma_start(o["ssd_conv_prompt"][0, 0], crows[0:3, :]).then_inc(sem("crow_stored"), 16)
            act.dma_start(o["ssd_conv_sample"][0, :, 2, :], crows[3:11, :]).then_inc(sem("crow_stored"), 16)
            act.wait_ge(sem("adt_ready"), 1)
            a.activation(dtx[0:TS, 16:32], adt[0:TS, 32:48], ACT.Exp).then_inc(sem("sda_ready"), 1)

            def sample_bc(k):
                if k >= 2:
                    act.wait_ge(sem("t2_ready"), k - 1)
                    act.wait_ge(sem("sy_mul"), k - 1)
                for j in range(2):
                    filled(act, ("BC", 2 * k + j))
                    a.activation(BCr[:, j, 512 * (k % 2):512 * (k % 2) + 512], tile(("BC", 2 * k + j))[:, :],
                                 ACT.Copy).then_inc(sem("bc_ready"), 1)

            for c in range(DC):
                filled(act, ("v", c))
                a.activation(GV[:, c, :], tile(("v", c))[:, 0:T], ACT.Gelu_apprx_tanh).then_inc(sem("gv_ready"), 1)
                if c >= 4:
                    sample_bc(c - 4)
                if c == 3:
                    for k in range(2):
                        filled(act, ("sBC", k))
                        a.activation(sBC[:, 512 * k:512 * (k + 1)], tile(("sBC", k))[0:TS, :], ACT.Copy).then_inc(
                            sem("sbc_ready"), 1)
                    filled(act, "dtT")
                    a.activation(dts[0:HEADS, :], tile("dtT")[0:HEADS, 0:16], ACT.Copy).then_inc(sem("dtT_ready"), 1)
            for k in range(DC):
                filled(act, ("u", k))
                a.activation(U[:, k, :], tile(("u", k))[:, 0:T], ACT.Gelu_apprx_tanh).then_inc(sem("u_ready"), 1)
                if k < 4:
                    sample_bc(4 + k)
            for c in range(DC):
                act.wait_ge(sem("gv_cent"), c + 1)
                a.activation(SQ1[:, c, :], GV[:, c, :], ACT.Square).then_inc(sem("vsq_ready"), 1)
            root("lnv_var", 1)
            act.wait_ge(sem("tot_ready"), 2)
            a.activation(wend, wend, ACT.Exp).then_inc(sem("wend_ready"), 1)
            a.activation(wfin, wfin, ACT.Exp).then_inc(sem("wend_ready"), 1)
            for q in range(2):
                filled(act, ("Btok", q))
                a.activation(Btok[:, q, :], tile(("Btok", q))[:, :], ACT.Copy).then_inc(sem("btok_ready"), 1)
            for k in range(2):
                filled(act, ("vrow", k))
                a.activation(vrows[:, 512 * k:512 * (k + 1)], tile(("vrow", k))[0:TS, :], ACT.Copy).then_inc(
                    sem("vrow_ready"), 1)
            act.wait_ge(sem("vrow_ready"), 2)
            act.dma_start(o["gmlp_v"][0].rearrange("b s d -> (b s) d"), vrows).then_inc(sem("vrow_stored"), 16)
            for k in range(4):
                filled(act, ("vtok", k))
                a.activation(vtok[:, k // 2, 512 * (k % 2):512 * (k % 2) + 512], tile(("vtok", k))[:, :],
                             ACT.Copy).then_inc(sem("vtok_ready"), 1)
            for k in range(2):
                filled(act, ("prevT", k))
                a.activation(prevT[:, 512 * k:512 * (k + 1)], tile(("prevT", k))[:, :], ACT.Copy).then_inc(
                    sem("prevT_ready"), 1)
            for k in range(8):
                filled(act, ("z", k))
                a.activation(Z[:, k, :], tile(("z", k))[:, 0:T], ACT.Copy).then_inc(sem("z_raw"), 1)
                act.wait_ge(sem("seg_ready"), 4 * k + 4)
                a.activation(dec[:, k % 2], dec[:, k % 2], ACT.Exp).then_inc(sem("dec_ready"), 1)
                if k >= 4:
                    if k >= 6:
                        act.wait_ge(sem("cs_scaled"), k - 5)
                    a.activation(ecs[:, k % 2], tile(("cr", k))[:, :].rearrange("p (r l) -> p r l", r=4),
                                 ACT.Exp).then_inc(sem("ecs_ready"), 1)
            act.wait_ge(sem("z_raw"), 8)
            a.activation(Z, Z, ACT.Silu).then_inc(sem("z_ready"), 1)
            for k in range(2):
                filled(act, ("fst", k))
                a.activation(fsto[:, 512 * k:512 * (k + 1)], tile(("fst", k))[:, :], ACT.Copy).then_inc(
                    sem("fst_ready"), 1)
            act.wait_ge(sem("fst_ready"), 2)
            act.dma_start(o["ssm_prompt"][0, 0].rearrange("(c r) p n -> (r p) c n", r=2),
                          fsto.rearrange("p (c n) -> p c n", c=DC)).then_inc(sem("fst_stored"), 16)
            for c in range(DC):
                act.wait_ge(sem("gated"), c + 1)
                a.activation(SQ1[:, c, :], Z[:, c, :], ACT.Square).then_inc(sem("gsq_ready"), 1)
            for g in range(GR):
                filled(act, ("gn", g))
                if g >= 2:
                    act.wait_ge(sem("yn_ready"), 2 * g - 2)
                a.activation((rstd, muS)[g % 2][:, :], tile(("gn", g))[:, 0:T], ACT.Sqrt, scale=1.0 / 256,
                             bias=eps[:, 0:1]).then_inc(sem("gn_read"), 1)
            for c in range(DC):
                square(1, c, SQ2)
            root("norm1", 0)
            crd = i["state_conf_conv"][0].rearrange("(s b) k d -> (b k) s d", s=2)
            for b in range(4):
                act.wait_ge(sem(f"st_stored{b}"), 32)
            act.dma_start(ccr[0:120], crd).then_inc(sem("ccr_loaded"), 16)
            for f in range(FC):
                filled(act, ("fg", f))
                if f >= 2:
                    act.wait_ge(sem("fh_ready"), f - 1)
                a.activation(siluG[:, f % 2, :], tile(("fg", f))[:, 0:T], ACT.Silu).then_inc(sem("fg_ready"), 1)
            for c in range(DC):
                square(2, c, SQ2)
            root("norm2", 0)
            for k in range(4):
                filled(act, ("cbT", k))
                a.activation(ccb[:, 480 * k:480 * (k + 1)], tile(("cbT", k))[:, 0:480], ACT.Copy).then_inc(
                    sem("ccb_ready"), 1)

            def diagonal(n):
                c, k = PE_CHUNKS[n // KC], n % KC
                w = COL["conf_dw_w"] + 8 * k + c
                if n >= DIAGS:
                    act.wait_ge(sem("taps_used"), n - DIAGS + 1)
                a.activation(diag[:, n % DIAGS, :], ident[:, :], ACT.Copy, scale=par[:, w:w + 1]).then_inc(
                    sem("diag_ready"), 1)

            for c in range(DC):
                filled(act, ("cg", c))
                if c >= 2:
                    act.wait_ge(sem("ca_ready"), c - 1)
                bcol = COL["conf_b1"] + 8 + c
                a.activation(sgb[:, c % 2, :], tile(("cg", c))[:, 0:T], ACT.Sigmoid,
                             bias=par[:, bcol:bcol + 1]).then_inc(sem("sg_ready"), 1)
                for n in range(8 * c, min(8 * c + 8, DIAGS)):
                    diagonal(n)
            for k in range(2):
                filled(act, ("crw", k))
                a.activation(crw[0:38, 512 * k:512 * (k + 1)], tile(("crw", k))[0:38, :], ACT.Copy).then_inc(
                    sem("crw_ready"), 1)
            for n in range(DIAGS, KC * len(PE_CHUNKS)):
                diagonal(n)
            for n, c in enumerate(PE_CHUNKS):
                filled(act, ("taps", c))
                b = COL["conf_dw_b"] + c
                a.activation(CC[:, c, 0:TP], tile(("taps", c))[:, 0:TP], ACT.Identity, bias=par[:, b:b + 1]).then_inc(
                    sem("cc_taps"), 1)
            act.wait_ge(sem("crw_ready"), 2)
            act.dma_start(o["conf_conv_prompt"][0, 0], crw[0:30, :]).then_inc(sem("crw_stored"), 16)
            act.dma_start(o["conf_conv_sample"][0, :, 29, :], crw[30:38, :]).then_inc(sem("crw_stored"), 16)
            for c in range(DC):
                act.wait_ge(sem("cc_cent"), c + 1)
                a.activation(SQ2[:, c, :], CC[:, c, :], ACT.Square).then_inc(sem("csq_ready"), 1)
            root("lnc_var", 1)
            for c in range(DC):
                act.wait_ge(sem("cc_norm"), c + 1)
                gcol, bcol = COL["conf_ln_g"] + c, COL["conf_ln_b"] + c
                a.activation(CC[:, c, :], CC[:, c, :], ACT.Silu, bias=par[:, bcol:bcol + 1],
                             scale=par[:, gcol:gcol + 1]).then_inc(sem("cc_ready"), 1)
            for c in range(DC):
                square(3, c, SQ2)
            root("norm3", 0)
            for k in range(6):
                filled(act, ("xt2", k))
                n = ROWS[k // 2]
                a.activation(acc[0:n, k // 2, 512 * (k % 2):512 * (k % 2) + 512], tile(("xt2", k))[0:n, :],
                             ACT.Copy).then_inc(sem("acc_ready"), 1)
            for k in range(6):
                filled(act, ("ht", k))
                if k == 4:
                    act.wait_ge(sem("moe_zero"), 1)
                n = ROWS[k // 2]
                a.activation(htok[0:n, k // 2, 512 * (k % 2):512 * (k % 2) + 512], tile(("ht", k))[0:n, :],
                             ACT.Copy).then_inc(sem("htok_ready"), 1)
            act.wait_ge(sem("gate_diff"), 1)
            a.activation(gt12[:, 0:3], v12[:, 0:3], ACT.Exp).then_inc(sem("gate_exp"), 1)

            act.wait_ge(sem("rounds_ready"), 1)
            items = act.value_load(tint[0:1, 0:1], min_val=EXP, max_val=ITEMS)
            act.wait_ge(sem("gathered"), 1)
            a.activation(xg[:, 0:4], psum[4][:, 0:4 * CAP].rearrange("p (c j) -> p c j", c=4),
                         ACT.Copy).then_inc(sem("xg_lo"), 1)
            with act.Fori(0, items) as t:
                for k in range(LOADS):
                    act.wait_ge(sem("gu_full"), t * LOADS + (k + 1))
                    act.wait_ge(sem("moe_act"), t * LOADS + max(k, 1))
                    a.activation(sgm[:, k % 2], psum[k % 2][:, 0:2 * CAP].rearrange("p (f j) -> p f j", f=2),
                                 ACT.Silu).then_inc(sem("moe_silu"), 1)
                act.wait_ge(sem("gathered"), t + 2)
                a.activation(xg[:, 0:4], psum[4][:, 0:4 * CAP].rearrange("p (c j) -> p c j", c=4),
                             ACT.Copy).then_inc(sem("xg_lo"), 1)
                act.wait_ge(sem("w_used"), t * LOADS + LOADS)
                act.wait_ge(sem("scatter_full"), (t + 1) * 6)
                a.activation(ysb[0:CAP, 0:512], psum[2][0:CAP, :], ACT.Copy).then_inc(sem("ysb_lo"), 1)
            for k in range(BLK):
                n = ROWS[k]
                if k == 0:
                    act.wait_ge(sem("moe_scatter"), items * 6 + 7)
                else:
                    act.wait_ge(sem("fin_sq"), k)
                a.activation(fsq[0:n, :], acc[0:n, k, :], ACT.Square, accum_out=ssum[0:n, k:k + 1]).then_inc(
                    sem("fin_sq"), 1)
                act.wait_ge(sem("fin_sq"), k + 1)
                a.activation(ssum[0:n, k:k + 1], ssum[0:n, k:k + 1], ACT.Sqrt, scale=1.0 / D,
                             bias=eps[0:n, 0:1]).then_inc(sem("fin_root"), 1)
            yp = o["y_prompt"][0].rearrange("(k p) d -> p k d", p=P)
            for k in range(BLK):
                act.wait_ge(sem("out_ready"), k + 1)
                dst = yp[:, k] if k < 2 else o["y_sample"].rearrange("b s d -> (b s) d")
                act.dma_start(dst, acc[0:ROWS[k], k, :]).then_inc(sem("y_stored"), 16)

        @block.vector
        def _(dve):
            v = nc.vector
            order = [0]

            def then(ins):
                order[0] += 1
                ins.then_inc(sem("dve_step"), 1)
                dve.wait_ge(sem("dve_step"), order[0])

            def after(ins):
                order[0] += 1
                ins.then_inc(sem("dve_step"), 1)

            def reach():
                dve.wait_ge(sem("dve_step"), order[0])

            def col(name, c):
                return par[:, COL[name] + c:COL[name] + c + 1]

            def norm(k, gain):
                dve.wait_ge(sem("stat_read"), STATS.index(f"norm{k}") + 1)
                then(v.reciprocal(rstd[:, :], rstd[:, :]))
                for c in range(DC):
                    v.scalar_tensor_tensor(out=H[:, c, :], in0=XT[:, c, :], scalar=col(gain, c), in1=rstd[:, :],
                                           op0=ALU.mult, op1=ALU.mult).then_inc(sem("h_ready"), 1)

            v.memset(eps[:, 0:1], RMS_EPS).then_inc(sem("eps_ready"), 1)
            v.memset(eps[:, 1:2], LN_EPS).then_inc(sem("eps_ready"), 1)
            v.memset(prow[:, 0:4, :].rearrange("p k r -> p (k r)"), 0.0).then_inc(sem("prow_zero"), 1)
            after(v.memset(dtx, 0.0))
            after(v.memset(raw[:, :, 0:3], 0.0))
            for k in range(6):
                n = ROWS[k // 2]
                filled(dve, ("xT", k))
                src = tile(("xT", k))[:, :].rearrange("p (c t) -> p c t", c=4)[:, :, 0:n]
                v.tensor_copy(XT[:, 4 * (k % 2):4 * (k % 2) + 4, P * (k // 2):P * (k // 2) + n], src).then_inc(
                    sem("xT_ready"), 1)
            filled(dve, "par")
            v.tensor_copy(par[:, 0:192], tile("par")[:, 0:192]).then_inc(sem("par_ready"), 1)
            v.tensor_copy(par[:, 256:504], tile("par")[:, 256:504]).then_inc(sem("par_ready"), 1)
            filled(dve, "cols")
            v.tensor_copy(dfe, tile("cols")[:, 0:24]).then_inc(sem("cols_ready"), 1)
            dve.wait_ge(sem("xT_ready"), 6)
            dve.wait_ge(sem("par_ready"), 2)
            norm(0, "norm_mix_even")

            reach()
            for c in range(XBC):
                dve.wait_ge(sem("raw_ready"), c + 1)
                wk = [par[:, 128 + 16 * k + c:129 + 16 * k + c] for k in range(4)]
                dst = xc[:, c, 0:TP]
                then(v.tensor_scalar(dst, raw[:, c, 0:TP], wk[0], col("ssd_conv_b", c), ALU.mult, ALU.add))
                for k in range(1, 4):
                    ins = v.scalar_tensor_tensor(out=dst, in0=raw[:, c, k:k + TP], scalar=wk[k], in1=dst,
                                                 op0=ALU.mult, op1=ALU.add)
                    if k < 3:
                        then(ins)
                    else:
                        ins.then_inc(sem("conv_ready"), 1)
            dve.wait_ge(sem("cbuf_ready"), 1)
            xs = xc[:, :, TP:T]
            cbv = cbuf.rearrange("p c (b k) -> p c b k", b=TS)
            cwv = par[:, 128:192].rearrange("p (k c) -> p k c", k=4)
            sct = muS[:, 0:128].rearrange("p (c b) -> p c b", c=XBC)
            then(v.tensor_tensor(xs, raw[:, :, 3 + TP:3 + T], bc(cwv[:, 3], 2, [P, XBC, TS]), ALU.mult))
            for k in range(3):
                then(v.tensor_tensor(sct, cbv[:, :, :, k], bc(cwv[:, k], 2, [P, XBC, TS]), ALU.mult))
                then(v.tensor_tensor(xs, xs, sct, ALU.add))
            cb0 = COL["ssd_conv_b"]
            v.tensor_tensor(xs, xs, bc(par[:, cb0:cb0 + XBC], 2, [P, XBC, TS]), ALU.add).then_inc(
                sem("convs_ready"), 1)
            filled(dve, "dt")
            dve.wait_ge(sem("dtp_loaded"), 32)
            dps = tile("dt")[:, 0:48].rearrange("p (k h) -> p k h", k=BLK)
            dxv = dtx.rearrange("p (k h) -> p k h", k=BLK)
            v.tensor_tensor(dxv[:, 0:2], dps[:, 0:2], bc(dbias, 1, [P, 2, HEADS]), ALU.add).then_inc(sem("dt_raw"), 1)
            v.tensor_tensor(dxv[0:TS, 2], dps[0:TS, 2], dbias[0:TS, :], ALU.add).then_inc(sem("dt_raw"), 1)
            dve.wait_ge(sem("dt_act"), 3)
            then(v.tensor_scalar(dta, dtx, 0.0, None, ALU.max))
            then(v.tensor_tensor(dta, dta, dtm, ALU.add))
            dve.wait_ge(sem("arep_exp"), 1)
            v.scalar_tensor_tensor(out=adt.rearrange("p (k h) -> p k h", k=BLK),
                                   in0=dta.rearrange("p (k h) -> p k h", k=BLK), scalar=-1.0,
                                   in1=bc(arep, 1, [P, BLK, HEADS]), op0=ALU.mult, op1=ALU.mult).then_inc(
                sem("adt_ready"), 1)

            def layer_norm_mean(name, src, dst_sem):
                dve.wait_ge(sem("stat_full"), STATS.index(name) + 1)
                v.tensor_scalar(muS[:, :], STAT[:, 0:T], 1.0 / D, None, ALU.mult).then_inc(sem("stat_read"), 1)
                dve.wait_ge(sem("stat_read"), STATS.index(name) + 1)
                for c in range(DC):
                    v.tensor_tensor(src[:, c, :], src[:, c, :], muS[:, :], ALU.subtract).then_inc(sem(dst_sem), 1)

            def layer_norm_rstd(name):
                dve.wait_ge(sem("stat_read"), STATS.index(name) + 1)
                then(v.reciprocal(rstd[:, :], rstd[:, :]))

            reach()
            filled(dve, "dtrep")
            v.tensor_copy(dtrep, tile("dtrep")[:, 0:128]).then_inc(sem("dtrep_ready"), 1)
            drv = dtrep.rearrange("p (c k) -> p c k", c=DC)
            dve.wait_ge(sem("dtrep_ready"), 1)
            dve.wait_ge(sem("xc_ready"), XBC + 1)
            sxd = sdt[:, 128:192].rearrange("p (c b) -> p c b", c=DC)
            sy = sdt[:, 192:256].rearrange("p (c b) -> p c b", c=DC)
            then(v.tensor_tensor(sxd, xc[:, 0:DC, TP:T], drv[:, :, 0:TS], ALU.mult))

            def sample_in(k):
                dve.wait_ge(sem("bc_ready"), 2 * k + 1)
                v.tensor_tensor(
                    t2.rearrange("p (g r n) -> p g r n", g=GR, r=2),
                    bc(BCr[:, 0, 512 * (k % 2):512 * (k % 2) + 512].rearrange("p (g n) -> p g n", g=GR), 2, [P, GR, 2, NST]),
                    bc(sxd[:, :, k].rearrange("p (g r) -> p g r", r=2), 3, [P, GR, 2, NST]),
                    ALU.mult).then_inc(sem("t2_ready"), 1)
                dve.wait_ge(sem("t2_ready"), k + 1)
                dve.wait_ge(sem("st_decayed"), k + 1)
                now = st[:, k % 4]
                v.tensor_tensor(now, now, t2.rearrange("p (c n) -> p c n", c=DC), ALU.add).then_inc(sem("st_new"), 1)

            def sample_out(k):
                dve.wait_ge(sem("bc_ready"), 2 * k + 2)
                dve.wait_ge(sem("st_new"), k + 1)
                v.tensor_tensor(
                    t3.rearrange("p (g r n) -> p g r n", g=GR, r=2),
                    bc(BCr[:, 1, 512 * (k % 2):512 * (k % 2) + 512].rearrange("p (g n) -> p g n", g=GR), 2, [P, GR, 2, NST]),
                    st[:, k % 4].rearrange("p (g r) n -> p g r n", r=2), ALU.mult).then_inc(sem("sy_mul"), 1)
                dve.wait_ge(sem("sy_mul"), k + 1)
                then(v.tensor_reduce(sy[:, :, k], t3.rearrange("p (c n) -> p c n", c=DC), AX.X, ALU.add))

            for k in range(TS):
                sample_in(k)
                sample_out(k)
                if k == 3:
                    layer_norm_mean("lnv_mean", GV, "gv_cent")
            dve.wait_ge(sem("gv_cent"), DC)
            layer_norm_rstd("lnv_var")
            for c in range(DC):
                then(v.scalar_tensor_tensor(out=GV[:, c, :], in0=GV[:, c, :], scalar=col("gmlp_ln_g", c),
                                            in1=rstd[:, :], op0=ALU.mult, op1=ALU.mult))
                v.tensor_scalar(GV[:, c, :], GV[:, c, :], col("gmlp_ln_b", c), None, ALU.add).then_inc(
                    sem("vn_ready"), 1)

            filled(dve, "cs")
            after(v.tensor_scalar(tot, tile("cs")[:, 32:64], 1.0, None, ALU.mult))
            v.tensor_scalar(ncs, tile("cs")[:, 0:32], -1.0, None, ALU.mult).then_inc(sem("cs_ready"), 1)
            reach()
            dve.wait_ge(sem("cs_ready"), 1)
            v.tensor_tensor(wend, tot, ncs, ALU.add).then_inc(sem("tot_ready"), 1)
            dve.wait_ge(sem("tot_ready"), 1)
            v.tensor_tensor(wfin, wend[:, 0:16], tot[:, 16:32], ALU.add).then_inc(sem("tot_ready"), 1)
            for k in range(4):
                q, half = k // 2, k % 2
                filled(dve, ("xtok", k))
                v.tensor_tensor(xdt[:, q, 512 * half:512 * (half + 1)].rearrange("p (h d) -> p h d", h=8),
                                tile(("xtok", k))[:, :].rearrange("p (h d) -> p h d", h=8),
                                bc(dta[:, 16 * q + 8 * half:16 * q + 8 * half + 8], 2, [P, 8, HD]),
                                ALU.mult).then_inc(sem("xdt_ready"), 1)
            dve.wait_ge(sem("wend_ready"), 2)
            dve.wait_ge(sem("xdt_ready"), 4)
            hd = lambda ap: ap.rearrange("p (h d) -> p h d", h=HEADS)
            v.tensor_tensor(hd(xw0), hd(xdt[:, 0]), bc(wend[:, 0:16], 2, [P, HEADS, HD]), ALU.mult).then_inc(
                sem("xw_ready"), 1)
            dve.wait_ge(sem("crow_stored"), 32)
            v.tensor_tensor(hd(xf[:, 0]), hd(xdt[:, 0]), bc(wfin, 2, [P, HEADS, HD]), ALU.mult).then_inc(
                sem("xf_ready"), 1)
            v.tensor_tensor(hd(xf[:, 1]), hd(xdt[:, 1]), bc(wend[:, 16:32], 2, [P, HEADS, HD]), ALU.mult).then_inc(
                sem("xf_ready"), 1)
            dve.wait_ge(sem("cols_ready"), 1)
            sv = muS[:, 64:128].rearrange("p (c b) -> p c b", c=DC)
            then(v.tensor_tensor(sv, GV[:, :, TP:T], bc(dfe[:, 8:16], 2, [P, DC, TS]), ALU.mult))
            then(v.tensor_tensor(sv, sv, bc(dfe[:, 16:24], 2, [P, DC, TS]), ALU.add))
            for g in range(DC):
                filled(dve, ("mx", g))
                if g == 0:
                    dve.wait_ge(sem("u_ready"), DC)
                v.tensor_tensor(U[:, g, TP:T], U[:, g, TP:T], sv[:, g, :], ALU.mult).then_inc(sem("gout_ready"), 1)
                v.tensor_tensor(U[:, g, 0:TP], U[:, g, 0:TP], tile(("mx", g))[:, 0:TP], ALU.mult).then_inc(
                    sem("gout_ready"), 1)
            for k in range(9):
                if k < 8:
                    q, g = k // 4, k % 4
                    filled(dve, ("cr", k))
                    if k >= 2:
                        dve.wait_ge(sem("m_ready"), k - 1)
                    for r in range(4):
                        h = 4 * g + r
                        v.scalar_tensor_tensor(out=dec[:, k % 2, r], in0=tile(("cr", k))[:, P * r:P * (r + 1)],
                                               scalar=ncs[:, 16 * q + h:16 * q + h + 1], in1=negm[:, :],
                                               op0=ALU.add, op1=ALU.add).then_inc(sem("seg_ready"), 1)
                    dve.wait_ge(sem("dec_ready"), k + 1)
                    if k >= 2:
                        filled(dve, ("y", k - 2))
                    v.tensor_tensor(Mt[:, k % 2], dec[:, k % 2], bc(tile(("cb", k))[:, 0:P], 1, [P, 4, P]),
                                    ALU.mult).then_inc(sem("m_ready"), 1)
                    if q == 1:
                        dve.wait_ge(sem("ecs_ready"), g + 1)
                        v.tensor_tensor(Cs[:, k % 2], ecs[:, k % 2], bc(xc[:, 12 + g, P:TP], 1, [P, 4, P]),
                                        ALU.mult).then_inc(sem("cs_scaled"), 1)
                if k >= 1:
                    q, g = (k - 1) // 4, (k - 1) % 4
                    filled(dve, ("y", k - 1))
                    for r in range(2):
                        c = 2 * g + r
                        x = xc[:, c, P * q:P * (q + 1)]
                        v.scalar_tensor_tensor(out=x, in0=x, scalar=dfe[:, c:c + 1],
                                               in1=tile(("y", k - 1))[:, P * r:P * (r + 1)], op0=ALU.mult,
                                               op1=ALU.add).then_inc(sem("y_ready"), 1)
            xsm = xc[:, 0:DC, TP:T]
            then(v.tensor_tensor(xsm, xsm, bc(dfe[:, 0:8], 2, [P, DC, TS]), ALU.mult))
            then(v.tensor_tensor(xsm, xsm, sy, ALU.add))
            dve.wait_ge(sem("z_ready"), 1)
            dve.wait_ge(sem("y_ready"), 16)
            for c in range(DC):
                v.tensor_tensor(Z[:, c, :], Z[:, c, :], xc[:, c, :], ALU.mult).then_inc(sem("gated"), 1)
            for g in range(GR):
                root = (rstd, muS)[g % 2]
                dve.wait_ge(sem("gn_read"), g + 1)
                then(v.reciprocal(root[:, :], root[:, :]))
                for r in range(2):
                    c = 2 * g + r
                    ins = v.scalar_tensor_tensor(out=Z[:, c, :], in0=Z[:, c, :], scalar=col("ssd_norm", c),
                                                 in1=root[:, :], op0=ALU.mult, op1=ALU.mult)
                    ins.then_inc(sem("yn_ready"), 1)

            def residual(k, name, bias=None):
                for c in range(DC):
                    filled(dve, (name, c))
                    src = tile((name, c))[:, 0:T]
                    if bias:
                        ins = v.scalar_tensor_tensor(out=XT[:, c, :], in0=src, scalar=col(bias, c), in1=XT[:, c, :],
                                                     op0=ALU.add, op1=ALU.add)
                    else:
                        ins = v.tensor_tensor(XT[:, c, :], XT[:, c, :], src, ALU.add)
                    ins.then_inc(sem("res_ready"), 1)
                dve.wait_ge(sem("res_ready"), 8 * k + 8)

            residual(0, "wo")
            norm(1, "norm_ffn_even")
            for f in range(FC):
                filled(dve, ("fu", f))
                dve.wait_ge(sem("fg_ready"), f + 1)
                v.tensor_tensor(HT[:, f, :], siluG[:, f % 2, :], tile(("fu", f))[:, 0:T], ALU.mult).then_inc(
                    sem("fh_ready"), 1)
            residual(1, "fd")
            norm(2, "norm_mix_odd")
            then(v.memset(ca[:, :, 0:30], 0.0))
            for c in range(DC):
                filled(dve, ("cv", c))
                dve.wait_ge(sem("sg_ready"), c + 1)
                v.scalar_tensor_tensor(out=ca[:, c, 30:30 + T], in0=tile(("cv", c))[:, 0:T], scalar=col("conf_b1", c),
                                       in1=sgb[:, c % 2, :], op0=ALU.add, op1=ALU.mult).then_inc(sem("ca_ready"), 1)
                if c == 0:
                    dve.wait_ge(sem("ctmp_ready"), 1)
                    ctl = ctail.rearrange("p (c b) -> p c b", c=DC)
                    then(v.tensor_reduce(ctail, ctmp.rearrange("p (m k) -> p m k", k=30), AX.X, ALU.add))
                    bd = COL["conf_dw_b"]
                    then(v.tensor_tensor(ctl, ctl, bc(par[:, bd:bd + 8], 2, [P, DC, TS]), ALU.add))
                dve.wait_ge(sem("ca_ready"), c + 1)
                v.scalar_tensor_tensor(out=CC[:, c, TP:T], in0=ca[:, c, 30 + TP:30 + T],
                                       scalar=col("conf_dw_w", 240 + c), in1=ctl[:, c], op0=ALU.mult,
                                       op1=ALU.add).then_inc(sem("cc_samples"), 1)
                if c not in DVE_CHUNKS:
                    continue
                dst = CC[:, c, 0:TP]
                then(v.tensor_scalar(dst, ca[:, c, 0:TP], col("conf_dw_w", c), col("conf_dw_b", c), ALU.mult,
                                     ALU.add))
                for k in range(1, KC):
                    ins = v.scalar_tensor_tensor(out=dst, in0=ca[:, c, k:k + TP], scalar=col("conf_dw_w", 8 * k + c),
                                                 in1=dst, op0=ALU.mult, op1=ALU.add)
                    if k < KC - 1:
                        then(ins)
                ins.then_inc(sem("cc_conv"), 1)
            dve.wait_ge(sem("cc_samples"), DC)
            dve.wait_ge(sem("cc_conv"), len(DVE_CHUNKS))
            dve.wait_ge(sem("cc_taps"), len(PE_CHUNKS))
            dve.wait_ge(sem("cc_pool"), len(POOL_CHUNKS))
            layer_norm_mean("lnc_mean", CC, "cc_cent")
            dve.wait_ge(sem("cc_cent"), DC)
            layer_norm_rstd("lnc_var")
            for c in range(DC):
                v.tensor_tensor(CC[:, c, :], CC[:, c, :], rstd[:, :], ALU.mult).then_inc(sem("cc_norm"), 1)
            residual(2, "w2", "conf_b2")
            norm(3, "norm_ffn_odd")

            after(v.memset(htok[:, 2, :], 0.0))
            v.memset(SelGT[:, :], 0.0).then_inc(sem("moe_scatter"), 1)
            v.memset(hact[:, :, :, :].rearrange("p s f j -> p (s f j)"), 0.0).then_inc(sem("moe_act"), 1)
            v.memset(ysb[:, 0:512], 0.0).then_inc(sem("ysb_lo"), 1)
            v.memset(ysb[:, 512:1024], 0.0).then_inc(sem("ysb_hi"), 1)
            after(v.memset(rt[:, 700:900], -1000.0))
            then(v.memset(L, 0.0))
            v.memset(gtab.rearrange("p k n -> p (k n)"), 0.0).then_inc(sem("moe_zero"), 1)
            dve.wait_ge(sem("moe_zero"), 1)
            filled(dve, "lg")
            v.tensor_copy(L[:, 0:16], tile("lg")[:, 0:16]).then_inc(sem("lg_ready"), 1)
            v.tensor_copy(L[0:TS, 16:24], tile("lg")[0:TS, 16:24]).then_inc(sem("lg_ready"), 1)
            dve.wait_ge(sem("lg_ready"), 2)
            dve.wait_ge(sem("route_const"), 2)
            c1 = cmp1.rearrange("p (k e j) -> p k e j", k=BLK, e=EXP)
            c2 = cmp2.rearrange("p (k e j) -> p k e j", k=BLK, e=EXP)
            Lv = L.rearrange("p (k e) -> p k e", k=BLK)
            for k in range(BLK):
                lj = bc(Lv[:, k], 1, [P, EXP, EXP])
                le = bc(Lv[:, k], 2, [P, EXP, EXP])
                then(v.tensor_tensor(c1[:, k], lj, le, ALU.is_gt))
                then(v.tensor_tensor(c2[:, k], lj, le, ALU.is_equal))
                then(v.tensor_tensor(c2[:, k], c2[:, k], ltm.rearrange("p (e j) -> p e j", e=EXP), ALU.mult))
            then(v.tensor_tensor(cmp1, cmp1, cmp2, ALU.add))
            then(v.tensor_reduce(rank, cmp1.rearrange("p (m j) -> p m j", j=EXP), AX.X, ALU.add))
            k8 = lambda ap: ap.rearrange("p (k e) -> p k e", k=BLK)
            vb = bc(valid, 2, [P, BLK, EXP])
            then(v.tensor_scalar(m1, rank, 0.0, None, ALU.is_equal))
            then(v.tensor_scalar(m2, rank, 1.0, None, ALU.is_equal))
            then(v.tensor_tensor(k8(m1), k8(m1), vb, ALU.mult))
            then(v.tensor_tensor(k8(m2), k8(m2), vb, ALU.mult))
            v.tensor_tensor(mask, m1, m2, ALU.add).then_inc(sem("mask_ready"), 1)
            then(v.tensor_tensor(tmp24, L, m1, ALU.mult))
            then(v.tensor_reduce(v12[:, 3:6], k8(tmp24), AX.X, ALU.add))
            then(v.tensor_tensor(tmp24, L, m2, ALU.mult))
            then(v.tensor_reduce(v12[:, 0:3], k8(tmp24), AX.X, ALU.add))
            v.tensor_tensor(v12[:, 0:3], v12[:, 0:3], v12[:, 3:6], ALU.subtract).then_inc(sem("gate_diff"), 1)
            dve.wait_ge(sem("gate_exp"), 1)
            then(v.tensor_scalar(gt12[:, 3:6], gt12[:, 0:3], 1.0, None, ALU.add))
            then(v.reciprocal(gt12[:, 6:9], gt12[:, 3:6]))
            then(v.tensor_tensor(gt12[:, 9:12], gt12[:, 0:3], gt12[:, 6:9], ALU.mult))
            then(v.tensor_tensor(k8(m1), k8(m1), bc(gt12[:, 6:9], 2, [P, BLK, EXP]), ALU.mult))
            then(v.tensor_tensor(k8(m2), k8(m2), bc(gt12[:, 9:12], 2, [P, BLK, EXP]), ALU.mult))
            then(v.tensor_tensor(gate, m1, m2, ALU.add))
            filled(dve, "pos")
            dve.wait_ge(sem("mask_ready"), 1)
            after(v.tensor_copy(cnt, tile("pos")[:, 24:32]))
            v.tensor_scalar(posm, tile("pos")[:, 0:24], 1000.0, None, ALU.add).then_inc(sem("pos_ready"), 1)
            reach()
            dve.wait_ge(sem("pos_ready"), 1)
            then(v.tensor_tensor(posm, posm, mask, ALU.mult))
            for r in range(ROUNDS):
                after(v.tensor_scalar(ptab[:, :, 1 + EXP * r:1 + EXP * (r + 1)], k8(posm), -1000.0 - CAP * r, None,
                                      ALU.add))
                after(v.tensor_copy(gtab[:, :, 1 + EXP * r:1 + EXP * (r + 1)], k8(gate)))
            then(v.tensor_reduce(nrf[:, 0:1], cnt, AX.X, ALU.max))
            after(v.tensor_scalar(nrf[:, 1:2], nrf[:, 0:1], float(CAP), None, ALU.is_gt))
            then(v.tensor_scalar(nrf[:, 2:3], nrf[:, 0:1], float(2 * CAP), 1.0, ALU.is_gt, ALU.add))
            then(v.tensor_tensor(nrf[:, 0:1], nrf[:, 1:2], nrf[:, 2:3], ALU.add))
            after(v.tensor_scalar(tint[0:1, 0:1], nrf[0:1, 0:1], float(EXP), None, ALU.mult))
            reach()
            v.tensor_copy(tint[0:1, 1:2], nrf[0:1, 0:1]).then_inc(sem("rounds_ready"), 1)
            reach()

            def select(t):
                for b in range(BLK):
                    ins = v.tensor_scalar(Sel[:, b, :], iota[:, :], ptab[:, b, bass.ds(t + 1, 1)], None, ALU.is_equal)
                ins.then_inc(sem("sel_ready"), 1)

            def gather_out():
                v.tensor_copy(xg[:, 4:8], psum[5][:, 0:4 * CAP].rearrange("p (c j) -> p c j", c=4)).then_inc(
                    sem("xg_hi"), 1)

            def select_gates(t):
                for b in range(BLK):
                    ins = v.tensor_scalar(SelG[:, b, :], iota[:, :], ptab[:, b, bass.ds(t, 1)],
                                          gtab[:, b, bass.ds(t, 1)], ALU.is_equal, ALU.mult)
                ins.then_inc(sem("selg_ready"), 1)

            def scatter(t):
                dve.wait_ge(sem("selgT_full"), t + 1)
                v.tensor_copy(SelGT[0:CAP, :], psum[4][0:CAP, 0:BLK * P]).then_inc(sem("selgT_ready"), 1)
                for k in range(6):
                    n = ROWS[k // 2]
                    dve.wait_ge(sem("scatter_full"), t * 6 + (k + 1))
                    dst = acc[0:n, k // 2, 512 * (k % 2):512 * (k % 2) + 512]
                    v.tensor_tensor(dst, dst, psum[5 + k % 2][0:n, :], ALU.add).then_inc(sem("moe_scatter"), 1)

            items = dve.value_load(tint[0:1, 0:1], min_val=EXP, max_val=ITEMS)
            dve.wait_ge(sem("acc_ready"), 6)
            select(0)
            dve.wait_ge(sem("gathered"), 1)
            gather_out()
            with dve.Fori(0, items) as t:
                for k in range(LOADS):
                    if k == 0:
                        select_gates(t)
                    dve.wait_ge(sem("moe_silu"), t * LOADS + (k + 1))
                    if k >= 2:
                        dve.wait_ge(sem("w_used"), t * LOADS + (k - 1))
                    v.tensor_tensor(hact[:, k % 2], sgm[:, k % 2],
                                    psum[k % 2][:, 2 * CAP:4 * CAP].rearrange("p (f j) -> p f j", f=2),
                                    ALU.mult).then_inc(sem("moe_act"), 1)
                    if k == 3:
                        dve.wait_ge(sem("moe_scatter"), t * 6 + 1)
                        scatter(t)
                    if k == 7:
                        dve.wait_ge(sem("gathered"), t + 1)
                        select(t + 1)
                dve.wait_ge(sem("gathered"), t + 2)
                gather_out()
                dve.wait_ge(sem("w_used"), t * LOADS + LOADS)
                dve.wait_ge(sem("scatter_full"), (t + 1) * 6)
                v.tensor_copy(ysb[0:CAP, 512:1024], psum[3][0:CAP, :]).then_inc(sem("ysb_hi"), 1)
            select_gates(items)
            dve.wait_ge(sem("moe_scatter"), items * 6 + 1)
            scatter(items)
            dve.wait_ge(sem("moe_scatter"), items * 6 + 7)
            dve.wait_ge(sem("fgain_loaded"), 16)
            for k in range(BLK):
                n = ROWS[k]
                dve.wait_ge(sem("fin_root"), k + 1)
                r = ssum[0:n, k:k + 1]
                then(v.reciprocal(r, r))
                v.scalar_tensor_tensor(out=acc[0:n, k, :], in0=acc[0:n, k, :], scalar=r, in1=fgain[0:n, :],
                                       op0=ALU.mult, op1=ALU.mult).then_inc(sem("out_ready"), 1)

        @block.tensor
        def _(pe):
            mm, tr = nc.tensor.matmul, nc.tensor.transpose
            turn = [0]

            def claim(name):
                n = turn[0]
                assert TILES[n][0] == name, (TILES[n][0], name)
                turn[0] += 1
                if n >= RING:
                    for s, value in TILES[n - RING][1]:
                        pe.wait_ge(sem(s), value)
                return psum[n % RING]

            def done(ins):
                ins.then_inc(sem("psum_full"), 1)

            def weights(step):
                _, _, name, value = STEP[step]
                pe.wait_ge(sem(name), value)
                return wview(step)

            def project(name, w, cols, nk, src, fresh=None):
                ps = claim(name)
                for c in range(nk):
                    if fresh:
                        pe.wait_ge(sem(fresh[0]), fresh[1] + c + 1)
                    ins = mm(ps[:, 0:T], w[:, c, cols:cols + P], src[:, c, :], start=c == 0, stop=c == nk - 1)
                done(ins)

            def stat(name, ready, first, SQ, c, n=DC):
                k = STATS.index(name)
                if c == 0 and k:
                    pe.wait_ge(sem("stat_read"), k)
                pe.wait_ge(sem(ready), first + c + 1)
                ins = mm(STAT[:, 0:T], ones[:, :], SQ[:, c, :], start=c == 0, stop=c == n - 1)
                if c == n - 1:
                    ins.then_inc(sem("stat_full"), 1)

            pe.wait_ge(sem("ident_ready"), 1)
            pe.wait_ge(sem("x_loaded"), 48)
            for k in range(6):
                ps = claim(("xT", k))
                n = ROWS[k // 2]
                for j in range(4):
                    c = 4 * (k % 2) + j
                    ins = tr(ps[:, P * j:P * j + n], xtk[0:n, k // 2, P * c:P * (c + 1)], ident[0:n, 0:n])
                done(ins)
            pe.wait_ge(sem("ones_ready"), 1)
            for c in range(DC):
                stat("norm0", "sq_ready", 0, SQ0, c)
            pe.wait_ge(sem("par_loaded"), 16 * (len(PARAMS) + 3))
            ps = claim("par")
            for k in range(4):
                ins = tr(ps[:, P * k:P * (k + 1)], prow[:, k, :], ident[:, :])
            done(ins)
            pe.wait_ge(sem("esel_ready"), 1)
            pe.wait_ge(sem("row_loaded"), 48)
            ps = claim("cols")
            for c in range(DC):
                mm(ps[:, c:c + 1], esel[:, c, :], dts[0:HEADS, 0:1], start=True, stop=True)
            done(mm(ps[:, 8:24], ones[0:1, :], row16[0:1, :], start=True, stop=True))
            pe.wait_ge(sem("wsn_ready"), 1)
            for k in range(2):
                ps = claim(("wsT", k))
                for j in range(4):
                    ins = tr(ps[:, P * j:P * (j + 1)], wsn[:, 4 * k + j, :], ident[:, :])
                done(ins)
            pe.wait_ge(sem("cb_loaded"), 16)
            ps = claim("cbufT")
            for c in range(XBC):
                ins = tr(ps[:, 24 * c:24 * c + 24], cbrows[:, P * c:P * (c + 1)], ident[0:24, 0:24])
            done(ins)
            for s in range(4):
                w = weights(("in", 1024 + 512 * s)).rearrange("p (c n) -> p c n", c=DC)
                for j in range(4):
                    project(("xbc", 4 * s + j), w, P * j, DC, H, ("h_ready", 0) if s + j == 0 else None)
            pe.wait_ge(sem("wdt_loaded"), 16)
            ps = claim("dt")
            wd = wdt[:, :].rearrange("p (c n) -> p c n", c=DC)
            for k in range(BLK):
                n = ROWS[k]
                for c in range(DC):
                    ins = mm(ps[0:n, 16 * k:16 * k + 16], H[:, c, P * k:P * k + n], wd[:, c, :], start=c == 0,
                             stop=c == DC - 1)
            done(ins)
            pe.wait_ge(sem("raw_ready"), XBC)
            for k in range(4):
                ps = claim(("crow", k))
                for j in range(4):
                    ins = tr(ps[0:11, P * j:P * (j + 1)], raw[:, 4 * k + j, T - 8:T + 3], ident[:, :])
                done(ins)

            def sample_bc(k):
                for b in range(2):
                    if k == 0 and b == 0:
                        pe.wait_ge(sem("sbc_ready"), 2)
                        pe.wait_ge(sem("const_ready"), 5)
                    ps = claim(("BC", 2 * k + b))
                    done(mm(ps[:, :], bsel[:, k, :], sBC[:, 512 * b:512 * (b + 1)], start=True, stop=True))

            for s in range(2):
                w = weights(("in", 4112 + 512 * s)).rearrange("p (c n) -> p c n", c=DC)
                for j in range(4):
                    project(("v", 4 * s + j), w, P * j, DC, H)
                    if s == 1:
                        sample_bc(j)
                if s == 0:
                    pe.wait_ge(sem("xc_ready"), XBC + 1)
                    for k in range(2):
                        ps = claim(("sBC", k))
                        for g in range(GR):
                            ins = tr(ps[0:TS, P * g:P * (g + 1)], xc[:, 8 + 4 * k + g, TP:T], ident[:, :])
                        done(ins)
                    pe.wait_ge(sem("sda_ready"), 1)
                    ps = claim("dtT")
                    tr(ps[0:HEADS, 0:8], dta[0:TS, 32:48], ident[0:TS, 0:TS])
                    done(tr(ps[0:HEADS, 8:16], dtx[0:TS, 16:32], ident[0:TS, 0:TS]))
                    pe.wait_ge(sem("dtT_ready"), 1)
                    ps = claim("dtrep")
                    for c in range(DC):
                        ins = mm(ps[:, 16 * c:16 * c + 16], esel[:, c, :], dts[0:HEADS, :], start=True, stop=True)
                    done(ins)
            for s in range(2):
                w = weights(("in", 3088 + 512 * s)).rearrange("p (c n) -> p c n", c=DC)
                for j in range(4):
                    project(("u", 4 * s + j), w, P * j, DC, H)
                    if s == 0:
                        sample_bc(4 + j)
                    if s == 0 and j == 1:
                        for c in range(DC):
                            stat("lnv_mean", "gv_ready", 0, GV, c)
            for c in range(DC):
                stat("lnv_var", "vsq_ready", 0, SQ1, c)
            pe.wait_ge(sem("adt_ready"), 1)
            ps = claim("cs")
            mm(ps[:, 0:32], upper[:, :], adt[:, 0:32], start=True, stop=True)
            done(mm(ps[:, 32:64], ones[:, :], adt[:, 0:32], start=True, stop=True))
            pe.wait_ge(sem("xc_ready"), XBC + 1)
            for k in range(4):
                q, half = k // 2, k % 2
                ps = claim(("xtok", k))
                for j in range(4):
                    ins = tr(ps[:, P * j:P * (j + 1)], xc[:, 4 * half + j, P * q:P * (q + 1)], ident[:, :])
                done(ins)
            for q in range(2):
                ps = claim(("Btok", q))
                for g in range(GR):
                    ins = tr(ps[:, P * g:P * (g + 1)], xc[:, 8 + g, P * q:P * (q + 1)], ident[:, :])
                done(ins)
            pe.wait_ge(sem("vn_ready"), DC)
            for k in range(2):
                ps = claim(("vrow", k))
                for j in range(4):
                    ins = tr(ps[0:TS, P * j:P * (j + 1)], GV[:, 4 * k + j, TP:T], ident[:, :])
                done(ins)
            for k in range(4):
                q, half = k // 2, k % 2
                ps = claim(("vtok", k))
                for j in range(4):
                    ins = tr(ps[:, P * j:P * (j + 1)], GV[:, 4 * half + j, P * q:P * (q + 1)], ident[:, :])
                done(ins)
            pe.wait_ge(sem("bs_loaded"), 16)
            pe.wait_ge(sem("wsT_ready"), 2)
            pe.wait_ge(sem("vtok_ready"), 4)
            for g in range(DC):
                ps = claim(("mx", g))
                for q in range(2):
                    mm(ps[:, P * q:P * (q + 1)], vtok[:, q, P * g:P * (g + 1)], wsT[:, P * g:P * (g + 1)], start=True,
                       stop=False)
                    ins = mm(ps[:, P * q:P * (q + 1)], ones[0:1, :], bsrow[0:1, P * g:P * (g + 1)], start=False,
                             stop=True)
                done(ins)
            pe.wait_ge(sem("xw_ready"), 1)
            pe.wait_ge(sem("btok_ready"), 2)
            for k in range(2):
                ps = claim(("prevT", k))
                for j in range(2):
                    g = 2 * k + j
                    ins = mm(ps[:, 256 * j:256 * (j + 1)], Btok[:, 0, P * g:P * (g + 1)], xw0[:, 256 * g:256 * (g + 1)],
                             start=True, stop=True)
                done(ins)
            for k in range(9):
                if k < 8:
                    q, g = k // 4, k % 4
                    w = weights(("in", 512 * (k // 4))).rearrange("p (c n) -> p c n", c=DC)
                    project(("z", k), w, P * (k % 4), DC, H)
                    ps = claim(("cb", k))
                    done(mm(ps[:, 0:P], xc[:, 8 + g, P * q:P * (q + 1)], xc[:, 12 + g, P * q:P * (q + 1)], start=True,
                            stop=True))
                    ps = claim(("cr", k))
                    for r in range(4):
                        h = 16 * q + 4 * g + r
                        ins = mm(ps[:, P * r:P * (r + 1)], adt[:, h:h + 1].broadcast_to([P, P]), upper[:, :],
                                 start=True, stop=True)
                    done(ins)
                if k >= 1:
                    q, g = (k - 1) // 4, (k - 1) % 4
                    s = (k - 1) % 2
                    ps = claim(("y", k - 1))
                    pe.wait_ge(sem("m_ready"), k)
                    if q == 1:
                        pe.wait_ge(sem("prevT_ready"), 2)
                        pe.wait_ge(sem("cs_scaled"), g + 1)
                    for r in range(4):
                        h = 4 * g + r
                        dst = ps[HD * (r % 2):HD * (r % 2) + HD, P * (r // 2):P * (r // 2 + 1)]
                        ins = mm(dst, xdt[:, q, HD * h:HD * (h + 1)], Mt[:, s, r, :], start=True, stop=q == 0)
                        if q == 1:
                            ins = mm(dst, prevT[:, HD * h:HD * (h + 1)], Cs[:, s, r, :], start=False, stop=True)
                    done(ins)
            pe.wait_ge(sem("xf_ready"), 2)
            for k in range(2):
                ps = claim(("fst", k))
                for j in range(4):
                    c = 4 * k + j
                    for q in range(2):
                        ins = mm(ps[:, P * j:P * (j + 1)], xf[:, q, P * c:P * (c + 1)],
                                 Btok[:, q, P * (c // 2):P * (c // 2 + 1)], start=q == 0, stop=q == 1)
                done(ins)
            pe.wait_ge(sem("gout_ready"), 16)
            AHEAD = 3
            for n in range(AHEAD):
                w = weights(("out", 256 * (n // 2))).rearrange("p (c n) -> p c n", c=XBC)
                at = NUM[("wo", n)]
                for sname, value in TILES[at - RING][1]:
                    pe.wait_ge(sem(sname), value)
                for c in range(DC, XBC):
                    mm(psum[at % RING][:, 0:T], w[:, c, P * (n % 2):P * (n % 2) + P], mix[:, c, :], start=c == DC,
                       stop=False)
            for g in range(GR):
                ps = claim(("gn", g))
                for r in range(2):
                    pe.wait_ge(sem("gsq_ready"), 2 * g + r + 1)
                    ins = mm(ps[:, 0:T], ones[:, :], SQ1[:, 2 * g + r, :], start=r == 0, stop=r == 1)
                done(ins)
            for s in range(4):
                w = weights(("out", 256 * s)).rearrange("p (c n) -> p c n", c=XBC)
                for j in range(2):
                    n = 2 * s + j
                    ps = claim(("wo", n))
                    chunks = list(range(DC)) if n < AHEAD else list(range(DC, XBC)) + list(range(DC))
                    for c in chunks:
                        if n == 0:
                            pe.wait_ge(sem("yn_ready"), c + 1)
                        ins = mm(ps[:, 0:T], w[:, c, P * j:P * j + P], mix[:, c, :],
                                 start=n >= AHEAD and c == DC, stop=c == DC - 1)
                    done(ins)
                    if 2 * s + j:
                        stat("norm1", "sq_ready", 8, SQ2, 2 * s + j - 1)
            stat("norm1", "sq_ready", 8, SQ2, DC - 1)
            for s in range(LOADS):
                w = weights(("ffn", s))
                for j in range(2):
                    for m, name in enumerate(("fg", "fu")):
                        project((name, 2 * s + j), w[:, 2048 * m:2048 * (m + 1)].rearrange("p (c n) -> p c n", c=DC),
                                P * j, DC, H, ("h_ready", DC) if s + j + m == 0 else None)
            pe.wait_ge(sem("fh_ready"), FC)
            for s in range(4):
                w = weights(("down", s))[:, 0:FC * 256].rearrange("p (c n) -> p c n", c=FC)
                for j in range(2):
                    project(("fd", 2 * s + j), w, P * j, FC, HT)
                    if 2 * s + j:
                        stat("norm2", "sq_ready", 16, SQ2, 2 * s + j - 1)
            stat("norm2", "sq_ready", 16, SQ2, DC - 1)
            pe.wait_ge(sem("ccr_loaded"), 16)
            for k in range(4):
                ps = claim(("cbT", k))
                for j in range(4):
                    c, half = 2 * k + j // 2, j % 2
                    ins = tr(ps[:, 120 * j:120 * (j + 1)], ccr[0:120, half, P * c:P * (c + 1)], ident[0:120, 0:120])
                done(ins)
            for s in range(4):
                w = weights(("conf1", s))
                for j in range(2):
                    for m, name in enumerate(("cv", "cg")):
                        project((name, 2 * s + j), w[:, 2048 * m:2048 * (m + 1)].rearrange("p (c n) -> p c n", c=DC),
                                P * j, DC, H, ("h_ready", 2 * DC) if s + j + m == 0 else None)
            pe.wait_ge(sem("ca_ready"), DC)
            for k in range(2):
                ps = claim(("crw", k))
                for j in range(4):
                    ins = tr(ps[0:38, P * j:P * (j + 1)], ca[:, 4 * k + j, TP:TP + 38], ident[:, :])
                done(ins)
            for n, c in enumerate(PE_CHUNKS):
                ps = claim(("taps", c))
                for k in range(KC):
                    pe.wait_ge(sem("diag_ready"), KC * n + k + 1)
                    ins = mm(ps[:, 0:TP], diag[:, (KC * n + k) % DIAGS, :], ca[:, c, k:k + TP], start=k == 0,
                             stop=k == KC - 1)
                    if k < KC - 1:
                        ins.then_inc(sem("taps_used"), 1)
                done(ins)
            order = (1, 2, 0, 4, 5, 3, 6, 7)
            pe.wait_ge(sem("stat_read"), STATS.index("lnc_mean"))
            pe.wait_ge(sem("cc_samples"), DC)
            for n, c in enumerate(order):
                if c in POOL_CHUNKS:
                    pe.wait_ge(sem("cc_pool"), POOL_CHUNKS.index(c) + 1)
                elif c in PE_CHUNKS:
                    pe.wait_ge(sem("cc_taps"), PE_CHUNKS.index(c) + 1)
                else:
                    pe.wait_ge(sem("cc_conv"), DVE_CHUNKS.index(c) + 1)
                ins = mm(STAT[:, 0:T], ones[:, :], CC[:, c, :], start=n == 0, stop=n == DC - 1)
            ins.then_inc(sem("stat_full"), 1)
            for c in range(DC):
                stat("lnc_var", "csq_ready", 0, SQ2, c)
            for s in range(2):
                w = weights(("conf2", s))[:, 0:4096].rearrange("p (c n) -> p c n", c=DC)
                for j in range(4):
                    project(("w2", 4 * s + j), w, P * j, DC, CC, ("cc_ready", 0) if s + j == 0 else None)
                    if 4 * s + j:
                        stat("norm3", "sq_ready", 24, SQ2, 4 * s + j - 1)
            stat("norm3", "sq_ready", 24, SQ2, DC - 1)
            pe.wait_ge(sem("res_ready"), 24)
            for k in range(6):
                ps = claim(("xt2", k))
                n = ROWS[k // 2]
                for j in range(4):
                    c = 4 * (k % 2) + j
                    ins = tr(ps[0:n, P * j:P * (j + 1)], XT[:, c, P * (k // 2):P * (k // 2) + n], ident[:, :])
                done(ins)
            pe.wait_ge(sem("h_ready"), 4 * DC)
            pe.wait_ge(sem("router_loaded"), 16)
            ps = claim("lg")
            wr = wrt[:, :].rearrange("p (c n) -> p c n", c=DC)
            for k in range(BLK):
                n = ROWS[k]
                for c in range(DC):
                    ins = mm(ps[0:n, 8 * k:8 * k + 8], H[:, c, P * k:P * k + n], wr[:, c, :], start=c == 0,
                             stop=c == DC - 1)
            done(ins)
            for k in range(6):
                ps = claim(("ht", k))
                n = ROWS[k // 2]
                for j in range(4):
                    c = 4 * (k % 2) + j
                    ins = tr(ps[0:n, P * j:P * (j + 1)], H[:, c, P * (k // 2):P * (k // 2) + n], ident[:, :])
                done(ins)
            pe.wait_ge(sem("mask_ready"), 1)
            ps = claim("pos")
            for k in range(BLK):
                mm(ps[:, 8 * k:8 * k + 8], supper[:, :], mask[:, 8 * k:8 * k + 8], start=True, stop=k == 0)
                for b in range(k):
                    mm(ps[:, 8 * k:8 * k + 8], ones[:, :], mask[:, 8 * b:8 * b + 8], start=False, stop=b == k - 1)
            for b in range(BLK):
                ins = mm(ps[:, 24:32], ones[:, :], mask[:, 8 * b:8 * b + 8], start=b == 0, stop=b == BLK - 1)
            done(ins)
            assert turn[0] == len(TILES)

            def gather(value):
                pe.wait_ge(sem("sel_ready"), value)
                for c in range(DC):
                    for b in range(BLK):
                        ins = mm(psum[4 + c // 4][:, CAP * (c % 4):CAP * (c % 4 + 1)], htok[:, b, P * c:P * (c + 1)],
                                 Sel[:, b, :], start=b == 0, stop=b == BLK - 1)
                ins.then_inc(sem("gathered"), 1)

            def scatter(t):
                pe.wait_ge(sem("selg_ready"), t + 1)
                pe.wait_ge(sem("xg_lo"), t + 1)
                for b in range(BLK):
                    ins = tr(psum[4][0:CAP, P * b:P * (b + 1)], SelG[:, b, :], ident[:, :])
                ins.then_inc(sem("selgT_full"), 1)

            def scatter_rows(t):
                pe.wait_ge(sem("selgT_ready"), t + 1)
                pe.wait_ge(sem("ysb_lo"), t + 1)
                pe.wait_ge(sem("ysb_hi"), t + 1)
                pe.wait_ge(sem("xg_hi"), t + 1)
                for k in range(6):
                    b, n = k // 2, ROWS[k // 2]
                    if k >= 2:
                        pe.wait_ge(sem("moe_scatter"), t * 6 + k)
                    mm(psum[5 + k % 2][0:n, :], SelGT[0:CAP, P * b:P * b + n],
                       ysb[0:CAP, 512 * (k % 2):512 * (k % 2) + 512], start=True, stop=True).then_inc(
                        sem("scatter_full"), 1)

            def up(t, k):
                w = ring[:, 6144 * (k % 4):6144 * (k % 4 + 1)]
                pe.wait_ge(sem(f"w_slot{k % 4}"), t * (48 * SLOT_USES[k % 4]) + (SLOT_BASE[k % 4] + 48 * (k // 4 + 1)))
                pe.wait_ge(sem("moe_act"), t * LOADS + max(k, 1))
                for m in range(2):
                    wm = w[:, 2048 * m:2048 * (m + 1)].rearrange("p (c n) -> p c n", c=DC)
                    for f in range(2):
                        at = CAP * (2 * m + f)
                        for c in range(DC):
                            ins = mm(psum[k % 2][:, at:at + CAP], wm[:, c, P * f:P * (f + 1)], xg[:, c, :],
                                     start=c == 0, stop=c == DC - 1)
                ins.then_inc(sem("gu_full"), 1)

            def down(t, k):
                w = ring[:, 6144 * (k % 4) + 4096:6144 * (k % 4 + 1)].rearrange("p (f n) -> p f n", f=2)
                pe.wait_ge(sem("moe_act"), t * LOADS + (k + 2))
                if k == 0:
                    pe.wait_ge(sem("ysb_lo"), t + 1)
                    pe.wait_ge(sem("ysb_hi"), t + 1)
                for f in range(2):
                    for h in range(2):
                        ins = mm(psum[2 + h][0:CAP, :], hact[:, k % 2, f, :], w[:, f, 512 * h:512 * (h + 1)],
                                 start=k == 0 and f == 0, stop=k == LOADS - 1 and f == 1)
                ins.then_inc(sem("w_used"), 1)

            for s, value in [x for _, dr in TILES[-RING:] for x in dr]:
                pe.wait_ge(sem(s), value)
            pe.wait_ge(sem("rounds_ready"), 1)
            items = pe.value_load(tint[0:1, 0:1], min_val=EXP, max_val=ITEMS)
            gather(1)

            with pe.Fori(0, items) as t:
                pe.wait_ge(sem("xg_lo"), t + 1)
                pe.wait_ge(sem("xg_hi"), t + 1)
                for k in range(LOADS):
                    up(t, k)
                    if k >= 1:
                        down(t, k - 1)
                    if k == 2:
                        scatter(t)
                    if k == 4:
                        scatter_rows(t)
                    if k == 8:
                        pe.wait_ge(sem("moe_scatter"), t * 6 + 7)
                        gather(t + 2)
                down(t, LOADS - 1)

            scatter(items)
            scatter_rows(items)


STATS = ("norm0", "lnv_mean", "lnv_var", "norm1", "norm2", "lnc_mean", "lnc_var", "norm3")

_INS = ['x_prompt', 'x_sample', 'state_ssm', 'state_ssd_conv', 'state_conf_conv', 'norm_mix_even', 'w_in_even',
        'ssd_conv_w', 'ssd_conv_b', 'ssd_dt_bias', 'ssd_a_log', 'ssd_d', 'ssd_norm', 'gmlp_ln_g', 'gmlp_ln_b',
        'gmlp_w_s', 'gmlp_b_s', 'w_out_even', 'norm_ffn_even', 'ffn_w_gate', 'ffn_w_up', 'ffn_w_down',
        'norm_mix_odd', 'conf_w1', 'conf_b1', 'conf_dw_w', 'conf_dw_b', 'conf_ln_g', 'conf_ln_b', 'conf_w2',
        'conf_b2', 'norm_ffn_odd', 'moe_router', 'moe_w_gate', 'moe_w_up', 'moe_w_down', 'final_norm']
_OUTS = [("y_prompt", (1, TP, D)), ("y_sample", (TS, 1, D)), ("ssm_prompt", (1, 1, HEADS, HD, NST)),
         ("ssd_conv_prompt", (1, 1, 3, XBC * P)), ("conf_conv_prompt", (1, 1, KC - 1, D)),
         ("ssm_sample", (1, TS, HEADS, HD, NST)), ("ssd_conv_sample", (1, TS, 3, XBC * P)),
         ("conf_conv_sample", (1, TS, KC - 1, D)), ("gmlp_v", (1, TS, 1, D))]


def kernel(**inputs):
    import numpy as _np
    import concourse.bacc as _bacc
    from concourse import mybir as _mybir
    from concourse.bass_utils import run_bass_kernel_spmd as _run

    nc = _bacc.Bacc("TRN2", target_bir_lowering=False, num_devices=1, dynamic_dma_scratch_size=8192)
    arrays, ins, outs = {}, {}, {}
    for name in _INS:
        a = _np.ascontiguousarray(inputs[name])
        arrays[f"in_{name}_dram"] = a
        ins[name] = nc.dram_tensor(f"in_{name}_dram", a.shape, _mybir.dt.from_np(a.dtype), kind="ExternalInput").ap()
    for name, shape in _OUTS:
        outs[name] = nc.dram_tensor(f"out_{name}_dram", shape, _mybir.dt.float32, kind="ExternalOutput").ap()
    build(nc, ins, outs)
    r = _run(nc, [arrays], core_ids=[0])
    return tuple(r.results[0][f"out_{name}_dram"] for name, _ in _OUTS)
```
